# Optimizing a Trainium2 kernel written in Bass

```python
import jax, jax.numpy as jnp
from jax import lax
import numpy as np

D_MODEL = 2048
BATCH = 1
SEQ = 256
DEPTH = 2

GRID_W = 64
CTX_LEN = 256
GLA_HEADS = 4
GLA_DK = 128
GLA_DV = 256
GATE_RANK = 16
GATE_NORM = 16.0
CHUNK = 64
FN_GROUPS = 4
FN_GROUP_W = 256
MIX_W = GLA_HEADS * GLA_DV + FN_GROUPS * FN_GROUP_W
Q_OFF = 0
K_OFF = Q_OFF + GLA_HEADS * GLA_DK
V_OFF = K_OFF + GLA_HEADS * GLA_DK
R_OFF = V_OFF + GLA_HEADS * GLA_DV
ZF_OFF = R_OFF + GLA_HEADS * GLA_DV
ZB_OFF = ZF_OFF + GATE_RANK
F_OFF = ZB_OFF + GATE_RANK
IN_W = F_OFF + FN_GROUPS * FN_GROUP_W
D_CONV = D_MODEL
CONV_W = 31
D_FF = -(-8 * D_MODEL // (3 * 256)) * 256
EPS = 1e-6

kernel_name = 'hybrid_gla_fnet_conformer_dit_block'

def _rms(x, g):
    xf = x.astype(jnp.float32)
    y = xf * lax.rsqrt(jnp.mean(xf * xf, axis=-1, keepdims=True) + EPS)
    return (y * g.astype(jnp.float32)).astype(x.dtype)

def _layer_norm(x, g, b):
    xf = x.astype(jnp.float32)
    xc = xf - jnp.mean(xf, axis=-1, keepdims=True)
    y = xc * lax.rsqrt(jnp.mean(xc * xc, axis=-1, keepdims=True) + EPS)
    return (y * g.astype(jnp.float32) + b.astype(jnp.float32)).astype(x.dtype)

def _modulate(h, shift, scale):
    return h * (1 + scale) + shift

def _pos_embed_2d(rows, d, dtype):
    r = jnp.repeat(jnp.arange(rows, dtype=jnp.float32), GRID_W)
    col = jnp.tile(jnp.arange(GRID_W, dtype=jnp.float32), rows)
    nq = d // 4
    omega = 1.0 / (10000.0 ** (jnp.arange(nq, dtype=jnp.float32) / nq))
    ar = r[:, None] * omega[None, :]
    ac = col[:, None] * omega[None, :]
    pe = jnp.concatenate([jnp.sin(ar), jnp.cos(ar), jnp.sin(ac), jnp.cos(ac)], axis=-1)
    return pe.astype(dtype)

def _heads(t, dh):
    bsz, n, _ = t.shape
    return t.reshape(bsz, n, -1, dh).transpose(0, 2, 1, 3).astype(jnp.float32)

def _flip(t):
    return jnp.flip(t, axis=2)

def _log_gate(z, w2, b2):
    return jax.nn.log_sigmoid((z @ w2 + b2).astype(jnp.float32)) / GATE_NORM

def _gla_chunked(q, k, v, g, s0):
    bsz, nh, n_tok, dk = q.shape
    dv = v.shape[-1]
    n_chunk = n_tok // CHUNK
    rs = lambda t: t.reshape(bsz, nh, n_chunk, CHUNK, t.shape[-1])
    qc, kc, vc, gc = rs(q), rs(k), rs(v), rs(g)
    b = jnp.cumsum(gc, axis=3)
    b_last = b[:, :, :, -1:, :]
    q_dec = qc * jnp.exp(b)
    k_inv = kc * jnp.exp(-b)
    k_tail = kc * jnp.exp(b_last - b)
    upto = jnp.tril(jnp.ones((CHUNK, CHUNK), dtype=bool))
    att = jnp.where(upto, jnp.einsum('bhnid,bhnjd->bhnij', q_dec, k_inv), 0.0)
    o_intra = jnp.einsum('bhnij,bhnjv->bhniv', att, vc)

    def step(s, inp):
        qd, kt, vv, dec = inp
        o = jnp.einsum('bhid,bhdv->bhiv', qd, s)
        s = dec[..., None] * s + jnp.einsum('bhjd,bhjv->bhdv', kt, vv)
        return s, o

    xs = (jnp.moveaxis(q_dec, 2, 0), jnp.moveaxis(k_tail, 2, 0), jnp.moveaxis(vc, 2, 0),
          jnp.moveaxis(jnp.exp(b_last[:, :, :, 0, :]), 2, 0))
    s_fin, o_inter = lax.scan(step, s0, xs)
    o = o_intra + jnp.moveaxis(o_inter, 0, 2)
    return o.reshape(bsz, nh, n_tok, dv), s_fin

def _gla_final_state(k, v, g):
    cum = jnp.cumsum(g, axis=2)
    w = jnp.exp(cum[:, :, -1:, :] - cum)
    return jnp.einsum('bhld,bhlv->bhdv', k * w, v)

def _bidir_gla(q, k, v, gf, gb, sf0, sb0):
    of, sf = _gla_chunked(q, k, v, gf, sf0)
    ob, sb = _gla_chunked(_flip(q), _flip(k), _flip(v), _flip(gb), sb0)
    return of + _flip(ob), sf, sb

def _fourier(f):
    bsz, n_tok, _ = f.shape
    fg = f.reshape(bsz, n_tok, FN_GROUPS, FN_GROUP_W).astype(jnp.float32)
    y = jnp.fft.fftn(fg, axes=(1, 3), norm='ortho').real
    return y.reshape(bsz, n_tok, FN_GROUPS * FN_GROUP_W).astype(f.dtype)

def _project(a, w_in, gw_f, gb_f, gw_b, gb_b):
    p = a @ w_in
    q = _heads(p[..., Q_OFF:K_OFF], GLA_DK) * (GLA_DK ** -0.5)
    k = _heads(p[..., K_OFF:V_OFF], GLA_DK)
    v = _heads(p[..., V_OFF:R_OFF], GLA_DV)
    gf = _heads(_log_gate(p[..., ZF_OFF:ZB_OFF], gw_f, gb_f), GLA_DK)
    gb = _heads(_log_gate(p[..., ZB_OFF:F_OFF], gw_b, gb_b), GLA_DK)
    return q, k, v, gf, gb, p[..., R_OFF:ZF_OFF], p[..., F_OFF:]

def _mixer_out(o, r, f, norm_g, w_out):
    on = o * lax.rsqrt(jnp.mean(o * o, axis=-1, keepdims=True) + EPS) * norm_g.astype(jnp.float32)
    bsz, nh, n_tok, dv = on.shape
    on = on.transpose(0, 2, 1, 3).reshape(bsz, n_tok, nh * dv).astype(r.dtype) * jax.nn.silu(r)
    return jnp.concatenate([on, _fourier(f)], axis=-1) @ w_out

def _gla_fourier_mixer(a, ac, w_in, gw_f, gb_f, gw_b, gb_b, norm_g, w_out, ctx_out):
    bsz = a.shape[0]
    zero = jnp.zeros((bsz, GLA_HEADS, GLA_DK, GLA_DV), jnp.float32)
    if ctx_out:
        qc, kc, vc, gfc, gbc, rc, fc = _project(ac, w_in, gw_f, gb_f, gw_b, gb_b)
        oc, sf, sb = _bidir_gla(qc, kc, vc, gfc, gbc, zero, zero)
        yc = _mixer_out(oc, rc, fc, norm_g, w_out)
    else:
        kc = _heads(ac @ w_in[:, K_OFF:V_OFF], GLA_DK)
        vc = _heads(ac @ w_in[:, V_OFF:R_OFF], GLA_DV)
        gfc = _heads(_log_gate(ac @ w_in[:, ZF_OFF:ZB_OFF], gw_f, gb_f), GLA_DK)
        gbc = _heads(_log_gate(ac @ w_in[:, ZB_OFF:F_OFF], gw_b, gb_b), GLA_DK)
        sf = _gla_final_state(kc, vc, gfc)
        sb = _gla_final_state(_flip(kc), _flip(vc), _flip(gbc))
        yc = None
    q, k, v, gf, gb, r, f = _project(a, w_in, gw_f, gb_f, gw_b, gb_b)
    o, _, _ = _bidir_gla(q, k, v, gf, gb, sf, sb)
    return _mixer_out(o, r, f, norm_g, w_out), yc

def _conformer_conv(a, w_pw1, b_pw1, w_dw, b_dw, ln_g, ln_b, w_pw2, b_pw2):
    u = a @ w_pw1 + b_pw1
    u = u[..., :D_CONV] * jax.nn.sigmoid(u[..., D_CONV:])
    u = lax.conv_general_dilated(u, w_dw[:, None, :].astype(u.dtype), window_strides=(1,),
                                 padding=[(CONV_W // 2, CONV_W // 2)],
                                 dimension_numbers=('NWC', 'WIO', 'NWC'),
                                 feature_group_count=D_CONV) + b_dw
    u = jax.nn.silu(_layer_norm(u, ln_g, ln_b))
    return u @ w_pw2 + b_pw2

def _swiglu(a, w_in, w_out):
    hg = a @ w_in
    return (jax.nn.silu(hg[..., :D_FF]) * hg[..., D_FF:]) @ w_out

def _ctx_read_later(i):
    return any(j % 2 == 0 for j in range(i + 1, DEPTH))

def setup_inputs(seed: int = 0) -> dict:
    key = jax.random.key(seed)
    ks = iter(jax.random.split(key, 40))
    nrm = lambda shape, scale: jax.random.normal(next(ks), shape, jnp.float32) * scale
    D = D_MODEL
    ne = (DEPTH + 1) // 2
    no = DEPTH // 2
    return {
        'x': nrm((BATCH, SEQ, D), 1.0),
        'c': nrm((BATCH, D), 1.0),
        'ctx': nrm((BATCH, CTX_LEN, D), 1.0),
        'c_ctx': nrm((D,), 1.0),
        'ada_w': nrm((DEPTH, D, 6 * D), 0.5 * D ** -0.5),
        'ada_b': nrm((DEPTH, 6 * D), 0.01),
        'norm_mix_g': 1.0 + nrm((DEPTH, D), 0.05),
        'norm_ffn_g': 1.0 + nrm((DEPTH, D), 0.05),
        'ffn_w_in': nrm((DEPTH, D, 2 * D_FF), D ** -0.5),
        'ffn_w_out': nrm((DEPTH, D_FF, D), D_FF ** -0.5),
        'gm_w_in': nrm((ne, D, IN_W), D ** -0.5),
        'gla_gate_w_fwd': nrm((ne, GATE_RANK, GLA_HEADS * GLA_DK), GATE_RANK ** -0.5),
        'gla_gate_b_fwd': nrm((ne, GLA_HEADS * GLA_DK), 0.1),
        'gla_gate_w_bwd': nrm((ne, GATE_RANK, GLA_HEADS * GLA_DK), GATE_RANK ** -0.5),
        'gla_gate_b_bwd': nrm((ne, GLA_HEADS * GLA_DK), 0.1),
        'gla_norm_g': 1.0 + nrm((ne, GLA_DV), 0.05),
        'gm_w_out': nrm((ne, MIX_W, D), MIX_W ** -0.5),
        'cv_w_pw1': nrm((no, D, 2 * D_CONV), D ** -0.5),
        'cv_b_pw1': nrm((no, 2 * D_CONV), 0.01),
        'cv_w_dw': nrm((no, CONV_W, D_CONV), CONV_W ** -0.5),
        'cv_b_dw': nrm((no, D_CONV), 0.01),
        'cv_ln_g': 1.0 + nrm((no, D_CONV), 0.05),
        'cv_ln_b': nrm((no, D_CONV), 0.01),
        'cv_w_pw2': nrm((no, D_CONV, D), D_CONV ** -0.5),
        'cv_b_pw2': nrm((no, D), 0.01),
        'final_norm_g': 1.0 + nrm((D,), 0.05),
    }

def reference(x, c, ctx, c_ctx, ada_w, ada_b, norm_mix_g, norm_ffn_g, ffn_w_in, ffn_w_out,
              gm_w_in, gla_gate_w_fwd, gla_gate_b_fwd, gla_gate_w_bwd, gla_gate_b_bwd,
              gla_norm_g, gm_w_out, cv_w_pw1, cv_b_pw1, cv_w_dw, cv_b_dw, cv_ln_g, cv_ln_b,
              cv_w_pw2, cv_b_pw2, final_norm_g):
    rows = x.shape[1] // GRID_W
    h = x + _pos_embed_2d(rows, D_MODEL, x.dtype)
    hc = ctx
    silu_c = jax.nn.silu(c)
    silu_cc = jax.nn.silu(c_ctx)
    for i in range(DEPTH):
        j = i // 2
        even = i % 2 == 0
        ctx_next = _ctx_read_later(i)
        m = [t[:, None, :] for t in jnp.split(silu_c @ ada_w[i] + ada_b[i], 6, axis=-1)]
        a = _modulate(_rms(h, norm_mix_g[i]), m[0], m[1])
        if even or ctx_next:
            mc = jnp.split(silu_cc @ ada_w[i] + ada_b[i], 6, axis=-1)
            ac = _modulate(_rms(hc, norm_mix_g[i]), mc[0], mc[1])
        if even:
            y, yc = _gla_fourier_mixer(a, ac, gm_w_in[j], gla_gate_w_fwd[j], gla_gate_b_fwd[j],
                                       gla_gate_w_bwd[j], gla_gate_b_bwd[j], gla_norm_g[j],
                                       gm_w_out[j], ctx_next)
        else:
            cv = (cv_w_pw1[j], cv_b_pw1[j], cv_w_dw[j], cv_b_dw[j], cv_ln_g[j], cv_ln_b[j],
                  cv_w_pw2[j], cv_b_pw2[j])
            y = _conformer_conv(a, *cv)
            yc = _conformer_conv(ac, *cv) if ctx_next else None
        h = h + m[2] * y
        h = h + m[5] * _swiglu(_modulate(_rms(h, norm_ffn_g[i]), m[3], m[4]), ffn_w_in[i], ffn_w_out[i])
        if ctx_next:
            hc = hc + mc[2] * yc
            hc = hc + mc[5] * _swiglu(_modulate(_rms(hc, norm_ffn_g[i]), mc[3], mc[4]),
                                      ffn_w_in[i], ffn_w_out[i])
    return _rms(h, final_norm_g)


_drawn_inputs = setup_inputs


def setup_inputs(seed=0):
    import zlib

    import numpy as np

    out = dict(_drawn_inputs(seed))
    spreads = {}
    factors = {'ctx': 3.382,
     'c_ctx': 5.523,
     'ada_b': 4.196,
     'norm_mix_g': 3.053,
     'norm_ffn_g': 3.162,
     'gla_gate_b_fwd': 8.0,
     'gla_gate_b_bwd': 7.218,
     'gla_norm_g': 8.0,
     'cv_b_pw1': 49.854,
     'cv_b_dw': 38.326,
     'cv_ln_g': 22.947,
     'cv_ln_b': 176.197,
     'cv_b_pw2': 64.0}
    for name, (base, spread) in spreads.items():
        noise = np.random.default_rng([zlib.crc32(name.encode()), seed]).standard_normal(out[name].shape)
        drawn = base * np.exp(spread * noise) if base else spread * noise
        out[name] = __import__('jax').numpy.asarray(drawn.astype(out[name].dtype))
    for name, factor in factors.items():
        out[name] = (out[name] * factor).astype(out[name].dtype)
    return out
```

```python
from contextlib import ExitStack

import concourse.bass as bass
from concourse import mybir

F32 = mybir.dt.float32
F32R = mybir.dt.float32r
U32 = mybir.dt.uint32
ALU = mybir.AluOpType
ACT = mybir.ActivationFunctionType

P = 128
D = 2048
KC = D // P
SEQ = 256
TT = SEQ // P
HEADS, DK, DV, CHUNK, RANK = 4, 128, 256, 64, 16
FN_W = 256
NW = 512
KS = 4
Q_OFF, K_OFF, V_OFF, R_OFF, Z_OFF, F_OFF = 0, 512, 1024, 2048, 3072, 3104
IN_W = 4128
D_FF = 5632
FB = D_FF // NW
CONV_W = 31
HALO = CONV_W // 2
EPS = 1e-6

SHIFT_MIX, SCALE_MIX, GATE_MIX, SHIFT_FFN, SCALE_FFN, GATE_FFN = range(6)
UNITS = 6 * D // NW

V_ADAB0, V_C, V_ADAB1, V_MIXG, V_FFNG, V_BDW, V_LNG, V_LNB, V_END = 0, 96, 128, 224, 256, 288, 304, 320, 336

(M_IDENT, M_INC_F, M_INC_B, M_AFTER, M_BEFORE, M_AFTER_ALL, M_BEFORE_ALL, M_ALL) = [P * n for n in range(8)]
M_PICK = P * 8
M_END = M_PICK + 2


class Ada:

    def __init__(self):
        self.slabs, self.pending = 0, 0

    def turned(self):
        was, self.pending = self.pending, 0
        return was

    def work(self, n):
        done = (self.slabs + n) // 4 - self.slabs // 4
        self.slabs += n
        self.pending |= done
        return done


class Tally:

    def __init__(self):
        self.n, self.per, self.it = 0, 0, None

    def at(self, more=0):
        return self.n + more if self.it is None else self.it * self.per + (self.n + more)

    def landed(self, ring):
        v = 16 * (self.n // ring + 1)
        return v if self.it is None else self.it * (16 * self.per // ring) + v


def loop(eng, count, *tallies_and_steps):
    with eng.Fori(0, count) as it:
        start = []
        for tally, per in tallies_and_steps:
            start.append(tally.n)
            tally.it, tally.per = it, per
        yield it
        for (tally, per), n in zip(tallies_and_steps, start):
            assert tally.n == n + per, (tally.n, n, per)
    for (tally, per), n in zip(tallies_and_steps, start):
        tally.n, tally.it = n + count * per, None


def program(nc, x, c, ctx, c_ctx, ada_w, ada_b, norm_mix_g, norm_ffn_g, ffn_w_in, ffn_w_out, gm_w_in,
            gate_w_f, gate_b_f, gate_w_b, gate_b_b, gla_norm_g, gm_w_out, cv_w_pw1, cv_b_pw1, cv_w_dw,
            cv_b_dw, cv_ln_g, cv_ln_b, cv_w_pw2, cv_b_pw2, final_norm_g, pos_embed, matrices, dft, out):
    with ExitStack() as stack:
        def sb(name, shape, dt=F32, on=stack):
            return on.enter_context(nc.sbuf_tensor(name, shape, dt))

        def sem(name):
            return stack.enter_context(nc.semaphore(name))

        w_raw = sb("w_raw", [P, 4, KS * NW])
        w_hi = sb("w_hi", [P, 2, KS * NW], F32R)
        w_lo = sb("w_lo", [P, 2, KS * NW], F32R)
        ada_raw = sb("ada_raw", [P, 2, KS * NW])
        a_hi = sb("a_hi", [P, KC, SEQ], F32R)
        a_lo = sb("a_lo", [P, KC, SEQ], F32R)
        mats = sb("mats", [P, M_END])
        ones = sb("ones", [P, P])
        mod = sb("mod", [P, 2 * 6 * KC, 2])
        vecs = sb("vecs", [P, V_END])
        w_dw = sb("w_dw", [P, KC, 32])
        c_pad = sb("c_pad", [P, KC, 32])
        ada_rows = sb("ada_rows", [P, NW])
        ssq = sb("ssq", [P, 8])
        rstd = sb("rstd", [P, 8])
        gain = sb("gain", [P, KC])
        gain_ctx = sb("gain_ctx", [P, KC])
        gla_g = sb("gla_g", [P, DV])
        arena0 = sb("arena0", [P, 20 * 256])
        with ExitStack() as early:
            ac_hi = sb("ac_hi", [P, KC, SEQ], F32R, early)
            ac_lo = sb("ac_lo", [P, KC, SEQ], F32R, early)
        with ExitStack() as late:
            hid_hi = sb("hid_hi", [P, KS, SEQ], F32R, late)
            hid_lo = sb("hid_lo", [P, KS, SEQ], F32R, late)
        arena1 = sb("arena1", [P, 32 * 256])
        arena2 = sb("arena2", [P, 28 * 256])

        def part(arena, kib, *shape):
            n = 1
            for d in shape:
                n *= d
            flat = arena[:, int(kib * 256):int(kib * 256) + n]
            if len(shape) == 1:
                return flat
            names = "abcd"[:len(shape)]
            return flat.rearrange(f"p ({' '.join(names)}) -> p {' '.join(names)}",
                                  **{k: v for k, v in zip(names[1:], shape[1:])})

        x_in = part(arena0, 0, TT, D)
        ctx_in = part(arena2, 0, TT, D)
        pe_in = part(arena1, 0, TT, D)
        dw_stage = part(arena1, 16, D)
        vec_stage = part(arena1, 24, 3, P)
        a32_mix = part(arena2, 16, 2, 2, SEQ)
        k_tok = part(arena0, 0, TT, 512)
        v_tok = part(arena0, 4, TT, 1024)
        g_tok = part(arena0, 12, TT, 2, 512)
        kc_tok = part(arena2, 0, TT, 512)
        vc_tok = part(arena2, 4, TT, 1024)
        gc_tok = part(arena2, 12, TT, 2, 512)
        z_aug = part(arena2, 20, 2 * SEQ)
        w2 = part(arena2, 22, 2, 512)
        gate_tmp = part(arena2, 26, 512)
        ctx_state = part(arena1, 0, HEADS, 2, DV)
        kc_tail = part(arena1, 8, TT, 2, 512)
        q_tok = part(arena1, 8, TT, 512)
        k_tail = part(arena1, 16, TT, 2, 512)
        qT = part(arena1, 24, HEADS, SEQ)
        kT = part(arena1, 28, HEADS, SEQ)
        r_tok = part(arena2, 0, TT, 1024)
        f_tok = part(arena2, 8, TT, 1024)
        qd = part(arena2, 16, 2, SEQ)
        ki = part(arena2, 18, 2, SEQ)
        states = part(arena2, 20, 2, 3, DV)
        att = part(arena2, 26, 2, TT, P)
        dec = part(arena1, 15.5, 2, 4)
        dft_cs = part(arena0, 0, 2, 512)
        dft_ns = part(arena1, 24, 2, FN_W)
        o_tmp = part(arena1, 12, TT, DV)
        o_dump = part(arena1, 14, DV)
        fn_cs = part(arena2, 16, 2, 2, 512)
        h = part(arena0, 0, TT, D)
        sg = part(arena0, 16, TT, NW)
        pe_out = part(arena1, 16, TT, D)
        gate_bc = part(arena1, 8, D)
        acc = part(arena1, 16, TT, D)
        conv_v = part(arena1, 16, KC, SEQ)
        uT = part(arena2, 0, KC, SEQ + 2 * HALO)
        sq = part(arena2, 0, KC, SEQ)
        b2_row = part(arena2, 0, D)
        fin_g = part(arena2, 0, D)
        b1_row = part(arena1, 8, 2, NW)
        hid_tok = part(arena2, 18, TT, NW)
        a32_ffn = part(arena2, 22, 2, 2, SEQ)
        prod = part(arena2, 22, 4, SEQ)
        pool_acc = part(arena2, 26, SEQ)
        mean_bc = part(arena2, 26, SEQ)
        rstd_bc = part(arena2, 27, SEQ)
        diag = part(arena2, 18, NW)

        A = [stack.enter_context(nc.psum_tensor(f"A{n}", [P, 512], F32)) for n in range(4)]
        O = [stack.enter_context(nc.psum_tensor(f"O{n}", [P, 512], F32)) for n in range(2)]
        T = stack.enter_context(nc.psum_tensor("T", [P, 512], F32))
        AD = stack.enter_context(nc.psum_tensor("AD", [P, 512], F32))

        w_landed = [sem(f"w_landed{n}") for n in range(4)]
        ada_landed = [sem(f"ada_landed{n}") for n in range(2)]
        start_landed = [sem(f"start_landed{n}") for n in range(5)]
        NAMES = """hi_ready lo_ready w_used ada_used rows_copied a_full tile_done a_free o_full o_free t_full
            t_free small_landed mats_landed x_landed ctx_landed cleared c_ready dve_step act_step x_ready
            ssq_ready hn_ready a32_even hi_done gain_ready z_ready w2_cleared w2_landed log_ready g_ready
            exp_ready qk_ready qd_ready att_ready sig_ready osq_ready gated dft_landed recip_ready y_hi root_ready h_landed
            diag_ready sg_ready hid_hi_ready h_ready b1_landed u_ready piece_done prod_ready prod_added conv_dve
            xc_ready sq_ready yn_ready ln_hi ln_lo b2_landed fin_landed result_ready stored start_used
            ada_summed""".split()
        (hi_ready, lo_ready, w_used, ada_used, rows_copied, a_full, tile_done, a_free, o_full, o_free, t_full,
         t_free, small_landed, mats_landed, x_landed, ctx_landed, cleared, c_ready, dve_step, act_step, x_ready,
         ssq_ready, hn_ready, a32_even, hi_done, gain_ready, z_ready, w2_cleared, w2_landed, log_ready, g_ready,
         exp_ready, qk_ready, qd_ready, att_ready, sig_ready, osq_ready, gated, dft_landed, recip_ready, y_hi, root_ready, h_landed,
         diag_ready, sg_ready, hid_hi_ready, h_ready, b1_landed, u_ready, piece_done, prod_ready, prod_added, conv_dve,
         xc_ready, sq_ready, yn_ready, ln_hi, ln_lo, b2_landed, fin_landed, result_ready, stored,
         start_used, ada_summed) = [sem(name) for name in NAMES]

        ident = mats[:, M_IDENT:M_IDENT + P]
        pick = mats[:, M_PICK:M_PICK + 2]

        def mat(m):
            return mats[:, m:m + P]

        def modc(layer, what, which=0):
            o = (layer * 6 + what) * KC
            return mod[:, o:o + KC, which]

        def rows(w):
            return w.rearrange("(k p) n -> p k n", p=P)

        gm_in, gm_out = rows(gm_w_in[0]), rows(gm_w_out[0])
        pw1, pw2 = rows(cv_w_pw1[0]), rows(cv_w_pw2[0])
        f_in = [rows(ffn_w_in[n]) for n in range(2)]
        f_out = [rows(ffn_w_out[n]) for n in range(2)]
        ada = [rows(ada_w[n]) for n in range(2)]

        def tiled(v):
            return v.rearrange("(t p) n -> p t n", p=P)

        MIX = [("k", K_OFF, True), ("v", V_OFF, True), ("v", V_OFF + NW, True), ("q", Q_OFF, False),
               ("r", R_OFF, False), ("r", R_OFF + NW, False), ("f", F_OFF, False), ("f", F_OFF + NW, False)]
        START_UNITS = 8
        START_ORDER = [s + m for m in range(4) for s in (0, 4)]
        START_RING = [ada_raw[:, 0, :], ada_raw[:, 1, :]] + [w_raw[:, n, :] for n in (1, 2, 3)]
        START_SLABS = 4 * START_UNITS

        def summed_by_dve(u):
            return 8 <= u < 14 or 23 <= u < 34

        DVE_SLABS, PE_SLABS = [0], [0]
        for u in range(START_UNITS, 2 * UNITS):
            for _ in range(4):
                DVE_SLABS.append(DVE_SLABS[-1] + summed_by_dve(u))
                PE_SLABS.append(PE_SLABS[-1] + (not summed_by_dve(u)))
        MIX_UNITS_END = 23
        ADA_FFN = (1, 0, 1, 0, 1, 0, 1, 0)
        ADA_PW1 = (0, 1, 2, 1, 1, 1, 2, 0)
        SLABS_TO_PW1 = 1 + (len(MIX) + 4) * (KC // KS) + FB * 12
        TURNS_TO_Y = 2 + START_UNITS + 10 + 4 + 2 * HEADS + 8
        A_MIX = (18, 22, 26, 30, 32, 35, 38, 41)
        SLABS = SLABS_TO_PW1 + 8 * 4 + 4 * 4 + FB * 12

        block = stack.enter_context(nc.Block())

        @block.sync
        def _(sp):
            S = Tally()

            def load(src):
                if S.it is not None or S.n >= 4:
                    sp.wait_ge(lo_ready, S.at(-3))
                elif S.n > 0:
                    sp.wait_ge(start_used, START_SLABS - 5 + S.n)
                dst = w_raw[:, S.n % 4, :].rearrange("p (k n) -> p k n", k=src.shape[1])
                sp.dma_start(dst, src).then_inc(w_landed[S.n % 4], 16)
                S.n += 1

            def column(w, n0, k0=0, slabs=KC // KS):
                for q in range(slabs):
                    load(w[:, k0 + KS * q:k0 + KS * (q + 1), n0:n0 + NW])

            def start_load(n):
                if n >= 5:
                    sp.wait_ge(start_used, n - 4)
                n0, q = START_ORDER[n // 4] * NW, n % 4
                sp.dma_start(START_RING[n % 5].rearrange("p (k n) -> p k n", k=KS),
                             ada[0][:, KS * q:KS * (q + 1), n0:n0 + NW]).then_inc(start_landed[n % 5], 16)

            sp.dma_start(mats[:, :], matrices).then_inc(mats_landed, 16)
            st = vec_stage
            for slot, r0, v in ((0, 0, ada_b[0]), (0, 96, c[0]), (0, 112, c_ctx), (1, 0, ada_b[1]),
                                (1, 96, norm_mix_g[0]), (1, 112, norm_mix_g[1]), (2, 0, norm_ffn_g[0]),
                                (2, 16, norm_ffn_g[1]), (2, 32, cv_b_dw[0]), (2, 48, cv_ln_g[0]),
                                (2, 64, cv_ln_b[0])):
                rws = v.shape[0] // P
                sp.dma_start(st[r0:r0 + rws, slot, :], v.rearrange("(r n) -> r n", n=P)).then_inc(small_landed, 16)
            for n in range(4):
                start_load(n)
            sp.wait_ge(cleared, 1)
            sp.dma_start(dw_stage[0:CONV_W, :], cv_w_dw[0]).then_inc(small_landed, 16)
            sp.dma_start(gla_g[:, :], gla_norm_g.broadcast_to([P, DV])).then_inc(small_landed, 16)
            sp.dma_start(x_in, tiled(x[0])).then_inc(x_landed, 16)
            sp.dma_start(pe_in, tiled(pos_embed)).then_inc(x_landed, 16)
            start_load(4)
            sp.dma_start(ctx_in, tiled(ctx[0])).then_inc(ctx_landed, 16)
            load(gm_in[:, :, Z_OFF:Z_OFF + P])
            for n in range(5, START_SLABS):
                start_load(n)
            for _, n0, _ in MIX:
                column(gm_in, n0)
            for m in range(4):
                column(gm_out, m * NW)
                if m == 0:
                    sp.wait_ge(gated, HEADS * TT)
                    sp.dma_start(dft_cs, dft[:, 0:512].rearrange("(t p) n -> p t n", p=P)).then_inc(dft_landed, 16)
                    sp.dma_start(dft_ns, dft[:, 512:768].rearrange("(t p) n -> p t n", p=P)).then_inc(dft_landed, 16)
                    sp.wait_ge(t_free, TURNS_TO_Y)
                    sp.dma_start(h, tiled(x[0])).then_inc(h_landed, 16)
                    sp.dma_start(pe_out, tiled(pos_embed)).then_inc(h_landed, 16)

            def ffn(layer):
                column(f_in[layer], 0)
                column(f_in[layer], D_FF)
                for i in loop(sp, FB - 1, (S, 12)):
                    for n0 in (0, D_FF):
                        for q in range(KC // KS):
                            load(f_in[layer][:, KS * q:KS * (q + 1), bass.ds(i * NW + (n0 + NW), NW)])
                    for m in range(4):
                        load(f_out[layer][:, bass.ds(i * KS, KS), m * NW:(m + 1) * NW])
                for m in range(4):
                    load(f_out[layer][:, KS * (FB - 1):KS * FB, m * NW:(m + 1) * NW])

            ffn(0)
            column(pw1, 0)
            column(pw1, D)
            for i in loop(sp, 3, (S, 8)):
                for n0 in (0, D):
                    for q in range(KC // KS):
                        load(pw1[:, KS * q:KS * (q + 1), bass.ds(i * NW + (n0 + NW), NW)])
            for m in range(4):
                column(pw2, m * NW)
                if m == 0:
                    sp.wait_ge(yn_ready, 4)
                    sp.dma_start(b2_row[0:1, :], cv_b_pw2).then_inc(b2_landed, 16)
            ffn(1)
            sp.wait_ge(h_ready, 3)
            sp.dma_start(fin_g, final_norm_g.rearrange("(a n) -> a n", a=1).broadcast_to([P, D])).then_inc(fin_landed, 16)
            for t in range(TT):
                sp.wait_ge(result_ready, t + 1)
                sp.dma_start(tiled(out[0])[:, t, :], h[:, t, :]).then_inc(stored, 16)
            sp.wait_ge(stored, 16 * TT)

        @block.gpsimd
        def _(pool):
            U = Tally()
            C = Tally()

            def ada_slab(src):
                n, it = U.n, U.it
                if n < 2:
                    pool.wait_ge(start_used, START_SLABS - 1 + n)
                elif summed_by_dve(START_UNITS + (n - 2) // 4):
                    used = 4 * DVE_SLABS[n - 1]
                    pool.wait_ge(ada_summed, used if it is None else it * (4 * U.per) + used)
                else:
                    used = PE_SLABS[n - 1]
                    pool.wait_ge(ada_used, used if it is None else it * U.per + used)
                dst = ada_raw[:, U.n % 2, :].rearrange("p (k n) -> p k n", k=KS)
                pool.dma_start(dst, src).then_inc(ada_landed[U.n % 2], 16)
                U.n += 1

            def unit(u, first=0, last=KC // KS):
                for q in range(first, last):
                    n0 = u % UNITS * NW
                    ada_slab(ada[u // UNITS][:, KS * q:KS * (q + 1), n0:n0 + NW])

            def unit_in_loop(n0):
                for q in range(KC // KS):
                    ada_slab(ada[1][:, KS * q:KS * (q + 1), bass.ds(n0, NW)])

            pool.wait_ge(w2_cleared, 1)
            pool.dma_start(w2[0:RANK, 0, :], gate_w_f[0]).then_inc(w2_landed, 16)
            pool.dma_start(w2[RANK:2 * RANK, 1, :], gate_w_b[0]).then_inc(w2_landed, 16)
            pool.dma_start(w2[2 * RANK:2 * RANK + 1, 0, :], gate_b_f).then_inc(w2_landed, 16)
            pool.dma_start(w2[2 * RANK:2 * RANK + 1, 1, :], gate_b_b).then_inc(w2_landed, 16)
            for u in range(START_UNITS, MIX_UNITS_END):
                unit(u)
            unit(MIX_UNITS_END)
            for i in loop(pool, FB - 1, (U, 4)):
                unit_in_loop(i * NW)

            def b1(cols, slabs_done):
                pool.wait_ge(w_used, slabs_done)
                for half in range(2):
                    pool.dma_start(b1_row[0:1, half, :], cv_b_pw1[:, cols(half * D)]).then_inc(b1_landed, 16)

            def add_products(first, last):
                for tap in range(max(first, 1), last):
                    pool.wait_ge(prod_ready, C.at(2 if tap == 1 else 1))
                    if tap == 1:
                        nc.gpsimd.tensor_tensor(pool_acc, prod[:, 0, :], prod[:, 1, :], ALU.add).then_inc(prod_added, 2)
                        C.n += 2
                    else:
                        pool.wait_ge(prod_added, C.at())
                        nc.gpsimd.tensor_tensor(pool_acc, pool_acc, prod[:, tap % 4, :], ALU.add).then_inc(prod_added, 1)
                        C.n += 1

            pool.wait_ge(h_ready, 2)
            b1(lambda o: slice(o, o + NW), SLABS_TO_PW1)
            unit(34)
            unit(35)
            for i in loop(pool, 3, (U, 8), (C, CONV_W)):
                b1(lambda o: bass.ds(i * NW + (NW + o), NW), i * 8 + (SLABS_TO_PW1 + 8))
                POOL_TAPS = [(0, 0)] * 4 + [(0, 6), (6, 11), (11, 16), (16, CONV_W)]
                for n in range(8):
                    col = i * (2 * NW) + (12 + n // 4) * NW
                    q = n % 4
                    ada_slab(ada[1][:, KS * q:KS * (q + 1), bass.ds(col, NW)])
                    add_products(*POOL_TAPS[n])
            unit(42, 0, 2)
            add_products(0, CONV_W)
            unit(42, 2, 4)
            for u in range(43, 48):
                unit(u)

        @block.tensor
        def _(pe):
            S, A_, O_, T_ = Tally(), Tally(), Tally(), Tally()
            U = Tally()
            G, V = Tally(), Tally()
            pending = [None]
            dft_bufs = [0]

            def take_a():
                if A_.n >= 4:
                    pe.wait_ge(a_free, A_.at(-3))
                A_.n += 1
                return A[(A_.n - 1) % 4]

            def take_o():
                if O_.n >= 2:
                    pe.wait_ge(o_free, O_.at(-1))
                O_.n += 1
                return O[(O_.n - 1) % 2]

            def take_t():
                if T_.n > 0:
                    pe.wait_ge(t_free, T_.at())
                T_.n += 1
                return T

            def products(bank, hi, lo, tile, k0, first, last):
                for k in range(KS):
                    wh = w_hi[:, S.n % 2, k * NW:(k + 1) * NW]
                    wl = w_lo[:, S.n % 2, k * NW:(k + 1) * NW]
                    ah = hi[:, k0 + k, tile * P:(tile + 1) * P]
                    al = lo[:, k0 + k, tile * P:(tile + 1) * P]
                    nc.tensor.matmul(bank, ah, wh, start=first and k == 0, stop=False)
                    nc.tensor.matmul(bank, ah, wl, start=False, stop=False)
                    mm = nc.tensor.matmul(bank, al, wh, start=False, stop=last and k == KS - 1)
                return mm

            def slab(banks, sources, k0, first, last, seeded=False, take=take_a):
                pe.wait_ge(lo_ready, S.at(1))
                for n, (hi, lo, tile) in enumerate(sources):
                    if first and not seeded:
                        banks.append(take())
                    mm = products(banks[n][:, :], hi, lo, tile, k0, first and not seeded, last)
                    if last and n < len(sources) - 1:
                        mm.then_inc(tile_done, 1)
                mm.then_inc(w_used, 1)
                S.n += 1

            def ada_work(slabs=1, bank_shared=False):
                for _ in range(slabs):
                    q = U.n % 4
                    if q == 0:
                        pe.wait_ge(rows_copied, G.at())
                        if bank_shared:
                            pe.wait_ge(t_free, T_.at())
                    pe.wait_ge(ada_landed[U.n % 2], U.landed(2))
                    for k in range(KS):
                        mm = nc.tensor.matmul(AD[32 * k:32 * k + 32, :], c_pad[:, KS * q + k, :],
                                              ada_raw[:, U.n % 2, k * NW:(k + 1) * NW], start=q == 0,
                                              stop=q == 3, tile_position=(0, 32 * k))
                    mm.then_inc(ada_used, 1)
                    U.n += 1
                    if q == 3:
                        G.n += 1
                        pending[0] = "pe"

            def ada_skip(slabs):
                U.n += slabs
                V.n += 4 * slabs
                if slabs and U.n % 4 == 0:
                    pending[0] = "dve"

            def ada_turn():
                who, pending[0] = pending[0], None
                if who is None:
                    return
                if who == "pe":
                    pe.wait_ge(rows_copied, G.at())
                else:
                    pe.wait_ge(ada_summed, V.at())
                bank = take_t()
                for m in range(4):
                    width, right = (2, pick) if who == "pe" else (1, ones[:, 0:1])
                    mm = nc.tensor.matmul(bank[:, width * m:width * (m + 1)], ada_rows[:, m * P:(m + 1) * P], right,
                                          start=True, stop=True)
                mm.then_inc(t_full, 1)

            def norm_turn(src, wait_sem, value, pairs=range(KC // 2)):
                pe.wait_ge(wait_sem, value)
                for j in pairs:
                    bank = take_a()
                    for e in range(2):
                        for t in range(TT):
                            k = 2 * j + e
                            mm = nc.tensor.transpose(bank[:, e * SEQ + t * P:e * SEQ + (t + 1) * P],
                                                     src[:, t, k * P:(k + 1) * P], ident)
                    mm.then_inc(a_full, 1)

            def gate_quarter(m, count):
                pe.wait_ge(diag_ready, count)
                bank = take_t()
                nc.tensor.matmul(bank[:, :], ones[:, :], diag, start=True, stop=True).then_inc(t_full, 1)

            pe.wait_ge(mats_landed, 16)
            pe.wait_ge(small_landed, 16 * 13)
            bank = take_t()
            for slot, n in ((0, P), (1, P), (2, V_END - 2 * P)):
                mm = nc.tensor.transpose(bank[:, slot * P:slot * P + n], vec_stage[0:n, slot, :], ident[0:n, 0:n])
            mm.then_inc(t_full, 1)
            bank = take_t()
            for k in range(KC):
                mm = nc.tensor.transpose(bank[:, 32 * k:32 * k + 32], dw_stage[0:32, k * P:(k + 1) * P],
                                         ident[0:32, 0:32])
            mm.then_inc(t_full, 1)
            pe.wait_ge(c_ready, 1)
            for n in range(START_SLABS):
                q = n % 4
                if q == 0 and n > 0:
                    pe.wait_ge(rows_copied, n // 4)
                pe.wait_ge(start_landed[n % 5], 16 * (n // 5 + 1))
                for k in range(KS):
                    mm = nc.tensor.matmul(AD[32 * k:32 * k + 32, :], c_pad[:, KS * q + k, :],
                                          START_RING[n % 5][:, k * NW:(k + 1) * NW], start=q == 0,
                                          stop=q == 3, tile_position=(0, 32 * k))
                mm.then_inc(start_used, 1)
                if q == 3:
                    G.n += 1
                    pending[0] = "pe"
                    ada_turn()
                if n % 8 == 7:
                    pairs = (n // 8 * 2, n // 8 * 2 + 1)
                    norm_turn(x_in, hn_ready, 2, pairs)
                    norm_turn(ctx_in, hn_ready, 4, pairs)

            lat = [(a_hi, a_lo, t) for t in range(TT)]
            both = lat + [(ac_hi, ac_lo, t) for t in range(TT)]

            pe.wait_ge(lo_ready, S.at(1))
            pe.wait_ge(a_free, A_.at())
            for n, (hi, lo) in enumerate(((a_hi, a_lo), (ac_hi, ac_lo))):
                bank = take_a()
                for k in range(KC):
                    wh = w_hi[:, S.n % 2, k * P:(k + 1) * P]
                    wl = w_lo[:, S.n % 2, k * P:(k + 1) * P]
                    nc.tensor.matmul(bank[:, 0:SEQ], wh, hi[:, k, :], start=k == 0, stop=False)
                    nc.tensor.matmul(bank[:, 0:SEQ], wh, lo[:, k, :], start=False, stop=False)
                    mm = nc.tensor.matmul(bank[:, 0:SEQ], wl, hi[:, k, :], start=False, stop=k == KC - 1)
                mm.then_inc(tile_done if n == 0 else w_used, 1)
            S.n += 1

            def gate_pre(n):
                t, d = n // 2, n % 2
                bank = take_o()
                nc.tensor.matmul(bank[:, :], z_aug[0:2 * RANK + 1, t * P:(t + 1) * P], w2[0:2 * RANK + 1, d, :],
                                 start=True, stop=True).then_inc(o_full, 1)

            def ctx_tails():
                pe.wait_ge(o_free, O_.at())
                for t in range(TT):
                    for d in range(2):
                        bank = take_o()
                        near = mat(M_BEFORE_ALL if d else M_AFTER_ALL)
                        far = t == d
                        mm = nc.tensor.matmul(bank[:, :], near, gc_tok[:, t, d, :], start=True, stop=not far)
                        if far:
                            mm = nc.tensor.matmul(bank[:, :], mat(M_ALL), gc_tok[:, 1 - t, d, :], start=False, stop=True)
                        mm.then_inc(o_full, 1)

            def ctx_states():
                pe.wait_ge(o_free, O_.at())
                for hd in range(HEADS):
                    bank = take_o()
                    for d in range(2):
                        for t in range(TT):
                            mm = nc.tensor.matmul(bank[:, d * DV:(d + 1) * DV], kc_tail[:, t, d, hd * DK:(hd + 1) * DK],
                                                  vc_tok[:, t, hd * DV:(hd + 1) * DV], start=t == 0, stop=t == 1)
                    mm.then_inc(o_full, 1)

            def lat_tails():
                for t in range(TT):
                    for d in range(2):
                        bank = take_o()
                        nc.tensor.matmul(bank[:, :], mat(M_BEFORE if d else M_AFTER), g_tok[:, t, d, :],
                                         start=True, stop=True).then_inc(o_full, 1)

            def turn_qk():
                for src in (q_tok, k_tok):
                    for t in range(TT):
                        bank = take_t()
                        for hd in range(HEADS):
                            mm = nc.tensor.transpose(bank[:, hd * P:(hd + 1) * P], src[:, t, hd * DK:(hd + 1) * DK], ident)
                        mm.then_inc(t_full, 1)

            def head_sums(hd):
                bank = take_t()
                for d in range(2):
                    for t in range(TT):
                        mm = nc.tensor.matmul(bank[:, d * SEQ + t * P:d * SEQ + (t + 1) * P],
                                              g_tok[:, t, d, hd * DK:(hd + 1) * DK], mat(M_INC_B if d else M_INC_F),
                                              start=True, stop=True)
                mm.then_inc(t_full, 1)

            def head_scores(hd):
                bank = take_t()
                for d in range(2):
                    for t in range(TT):
                        n = (d * TT + t) * P
                        mm = nc.tensor.matmul(bank[:, n:n + P], ki[:, d, t * P:(t + 1) * P], qd[:, d, t * P:(t + 1) * P],
                                              start=True, stop=True)
                mm.then_inc(t_full, 1)

            def head_update(hd, m):
                for d in range(2):
                    bank = take_o()
                    ch = 3 - m if d else m
                    t, r = ch // 2, CHUNK * (ch % 2)
                    mm = nc.tensor.matmul(bank[:, 0:DV], k_tail[r:r + CHUNK, t, d, hd * DK:(hd + 1) * DK],
                                          v_tok[r:r + CHUNK, t, hd * DV:(hd + 1) * DV], start=True, stop=True)
                    mm.then_inc(o_full, 1)

            def head_out(hd):
                pe.wait_ge(t_free, T_.at())
                pe.wait_ge(o_free, O_.at())
                bank = take_a()
                for t in range(TT):
                    ps = bank[:, t * DV:(t + 1) * DV]
                    for d in range(2):
                        nc.tensor.matmul(ps, att[:, d, t, :], v_tok[:, t, hd * DV:(hd + 1) * DV],
                                         start=t == 0 and d == 0, stop=False, skip_group_check=True)
                    for half in range(2):
                        ch = 2 * t + half
                        for d in range(2):
                            n = 3 - ch if d else ch
                            state = ctx_state[:, hd, d, :] if n == 0 else states[:, d, n - 1, :]
                            mm = nc.tensor.matmul(ps[half * CHUNK:(half + 1) * CHUNK, :],
                                                  qd[:, d, ch * CHUNK:(ch + 1) * CHUNK], state,
                                                  start=False, stop=d == 1, skip_group_check=True)
                mm.then_inc(a_full, 1)

            for n, (what, _, shared) in enumerate(MIX):
                banks = []
                for q in range(KC // KS):
                    slab(banks, both if shared else lat, KS * q, q == 0, q == 3)
                    ada_turn()
                    if n == 0:
                        if q == 0:
                            pe.wait_ge(a_free, A_.at(-4))
                            pe.wait_ge(w2_landed, 64)
                        gate_pre(2 * q)
                        gate_pre(2 * q + 1)
                    if n == 3:
                        (ctx_tails, ctx_states, lat_tails, lambda: None)[q]()
                    if n == 4 and q == 0:
                        pe.wait_ge(a_free, A_.at(-2))
                        turn_qk()
                    if n >= 4:
                        hd = n - 4
                        if q == 0:
                            head_sums(hd)
                        if q == 1:
                            head_scores(hd)
                            head_update(hd, 0)
                        if q == 2:
                            head_update(hd, 1)
                            head_update(hd, 2)
                        if q == 3:
                            head_out(hd)
                    if shared:
                        ada_skip(2)
                    else:
                        ada_work(1)

            pe.wait_ge(dft_landed, 32)
            for g in range(4):
                for dc in range(2):
                    bank = take_o()
                    if g == 0 and dc == 0:
                        pe.wait_ge(a_free, A_.at(-1))
                    for t in range(TT):
                        col = g * FN_W + dc * P
                        mm = nc.tensor.matmul(bank[:, :], f_tok[:, t, col:col + P], dft_cs[:, t, :], start=t == 0, stop=t == 1)
                    mm.then_inc(o_full, 1)
                pe.wait_ge(o_free, O_.at())
                bank = take_t()
                for e in range(2):
                    for dc in range(2):
                        nc.tensor.matmul(bank[:, e * SEQ:(e + 1) * SEQ], dft_cs[:, dc, e * P:(e + 1) * P],
                                         fn_cs[:, g % 2, dc, 0:SEQ], start=dc == 0, stop=False)
                        mm = nc.tensor.matmul(bank[:, e * SEQ:(e + 1) * SEQ], dft_ns[:, dc, e * P:(e + 1) * P],
                                              fn_cs[:, g % 2, dc, SEQ:2 * SEQ], start=False, stop=dc == 1)
                mm.then_inc(t_full, 1)
            pe.wait_ge(gated, HEADS * TT)
            for j in range(4):
                bank = take_t()
                for e in range(2):
                    for t in range(TT):
                        k = 2 * j + e
                        mm = nc.tensor.transpose(bank[:, e * SEQ + t * P:e * SEQ + (t + 1) * P],
                                                 r_tok[:, t, k * P:(k + 1) * P], ident)
                mm.then_inc(t_full, 1)
            pe.wait_ge(t_free, T_.at())
            assert T_.n == TURNS_TO_Y
            for m in range(4):
                banks = []
                for q in range(KC // KS):
                    slab(banks, lat, KS * q, q == 0, q == 3)
                    ada_turn()
                    if q == 0:
                        gate_quarter(m, m + 1)
                    ada_work(1)
            ada_turn()
            assert U.n == 4 * (MIX_UNITS_END - START_UNITS)

            hid = [(hid_hi, hid_lo, t) for t in range(TT)]

            def turn_hidden():
                pe.wait_ge(a_free, A_.at())
                for t in range(TT):
                    bank = T if t == 0 else AD
                    if t == 0:
                        take_t()
                    else:
                        T_.n += 1
                    for m in range(KS):
                        mm = nc.tensor.transpose(bank[:, m * P:(m + 1) * P], hid_tok[:, t, m * P:(m + 1) * P], ident)
                    mm.then_inc(t_full, 1)

            def ffn(layer, diags):
                norm_turn(acc, hn_ready, 6 if layer == 0 else 10)
                first = A_.n

                def block_in(head):
                    for half in range(2):
                        banks = []
                        for q in range(KC // KS):
                            if head and half == 0:
                                pe.wait_ge(a_free, first - 6 + 2 * q)
                            slab(banks, lat, KS * q, q == 0, q == 3)
                            if layer == 0:
                                ada_turn()
                                ada_skip(ADA_FFN[4 * half + q])

                block_in(True)
                turn_hidden()
                steps = [(S, 12), (A_, 4), (O_, 8)] + ([(T_, 3), (U, 4), (V, 16)] if layer == 0 else [(T_, 2)])
                for i in loop(pe, FB - 1, *steps):
                    block_in(False)
                    pe.wait_ge(t_free, T_.at(-1 if layer == 0 else 0))
                    for m in range(4):
                        slab([], hid, 0, True, True, take=take_o)
                    turn_hidden()
                pe.wait_ge(t_free, T_.at())
                for m in range(4):
                    slab([], hid, 0, True, True, take=take_o)
                    gate_quarter(m, diags + m + 1)

            ffn(0, 4)

            norm_turn(acc, hn_ready, 8)
            first = A_.n
            B = Tally()

            def turn_glu(t):
                bank = take_t()
                for m in range(KS):
                    mm = nc.tensor.transpose(bank[:, m * P:(m + 1) * P], hid_tok[:, t, m * P:(m + 1) * P], ident)
                mm.then_inc(t_full, 1)

            def pw1_block(head):
                for half in range(2):
                    banks = []
                    for q in range(KC // KS):
                        if q == 0:
                            if half == 0:
                                pe.wait_ge(b1_landed, B.at(32))
                            for t in range(TT):
                                banks.append(take_a())
                                nc.tensor.matmul(banks[t][:, :], ones[0:1, :], b1_row[0:1, half, :], start=True, stop=False)
                        if head and half == 0:
                            pe.wait_ge(a_free, first - 6 + 2 * q)
                        slab(banks, lat, KS * q, q == 0, q == 3, seeded=True)
                        n = half * 4 + q
                        ada_turn()
                        if not head and n in (1, 2):
                            if n == 1:
                                pe.wait_ge(a_free, A_.at(-2))
                            turn_glu(n - 1)
                        ada_work(ADA_PW1[n], bank_shared=n == 0)
                B.n += 32

            pw1_block(True)
            for i in loop(pe, 3, (S, 8), (A_, 4), (T_, 4), (U, 8), (G, 2), (B, 32)):
                pw1_block(False)
            pe.wait_ge(a_free, A_.at())
            for t in range(TT):
                turn_glu(t)
            bank = take_o()
            for k in range(KC):
                if k % KS == 0:
                    pe.wait_ge(conv_dve, CONV_W * (KS - 1) * (k // KS + 1))
                    pe.wait_ge(piece_done, k // KS + 1)
                mm = nc.tensor.matmul(bank[:, 0:SEQ], ones[:, :], conv_v[:, k, :], start=k == 0, stop=k == KC - 1)
            mm.then_inc(o_full, 1)
            bank = take_o()
            for k in range(KC):
                if k % KS == 0:
                    pe.wait_ge(sq_ready, k // KS + 1)
                mm = nc.tensor.matmul(bank[:, 0:SEQ], ones[:, :], sq[:, k, :], start=k == 0, stop=k == KC - 1)
            mm.then_inc(o_full, 1)
            for m in range(4):
                banks = []
                for q in range(KC // KS):
                    if m == 0:
                        pe.wait_ge(ln_lo, 2 * q + 2)
                    if q == 0:
                        if m == 0:
                            pe.wait_ge(b2_landed, 16)
                        for t in range(TT):
                            banks.append(take_a())
                            nc.tensor.matmul(banks[t][:, :], ones[0:1, :], b2_row[0:1, m * NW:(m + 1) * NW], start=True, stop=False)
                    slab(banks, lat, KS * q, q == 0, q == 3, seeded=True)
                    ada_turn()
                    if q == 0:
                        gate_quarter(m, 8 + m + 1)
                    ada_work(1 + (q + 1) % 2)
            ada_turn()
            assert U.n == 4 * (2 * UNITS - START_UNITS)
            ffn(1, 12)

        @block.scalar
        def _(act):
            S, W, D_, F, T_, O_ = Tally(), Tally(), Tally(), Tally(), Tally(), Tally()
            step = [0]
            W.n = -1

            def split():
                W.n += 1
                if S.n == SLABS:
                    return
                act.wait_ge(w_landed[S.n % 4], S.landed(4))
                if S.it is not None or S.n >= 2:
                    act.wait_ge(w_used, S.at(-1))
                nc.scalar.activation(w_hi[:, S.n % 2, :], w_raw[:, S.n % 4, :], ACT.Copy).then_inc(hi_ready, 1)
                S.n += 1

            def tile_ends(last):
                if last:
                    act.wait_ge(w_used, W.at())
                else:
                    act.wait_ge(tile_done, D_.at(1))
                    D_.n += 1

            def chained(ins):
                step[0] += 1
                ins.then_inc(act_step, 1)
                act.wait_ge(act_step, step[0])

            def root(v):
                R.n += 1
                act.wait_ge(recip_ready, R.n)
                nc.scalar.activation(v, v, ACT.Sqrt).then_inc(root_ready, 1)

            R = Tally()

            def sums_of_squares(src, dump, sem_, values, slot):
                for t in range(TT):
                    act.wait_ge(sem_, values[t])
                    nc.scalar.activation(dump[:, t, :], src[:, t, :], ACT.Square,
                                         accum_out=ssq[:, slot + t:slot + t + 1]).then_inc(ssq_ready, 1)
                root(rstd[:, slot:slot + TT])

            N = Tally()
            FREE = Tally()

            def norm_out(hi, add, a32, g=gain, pairs=range(KC // 2)):
                for j in pairs:
                    k = 2 * j + 1
                    act.wait_ge(a_full, F.at(1))
                    F.n += 1
                    if FREE.n >= 2:
                        act.wait_ge(a_free, FREE.n - 1)
                    N.n += 1
                    act.wait_ge(a32_even, N.n)
                    chained(nc.scalar.activation(a32[:, j % 2, 1, :], A[FREE.n % 4][:, SEQ:2 * SEQ], ACT.Identity,
                                                 bias=add[:, k:k + 1], scale=g[:, k:k + 1]))
                    nc.scalar.activation(hi[:, 2 * j:2 * j + 2, :], a32[:, j % 2, :, :], ACT.Copy).then_inc(hi_done, 1)
                    FREE.n += 1

            act.wait_ge(cleared, 3)
            nc.scalar.activation(c_pad[:, :, 0:2], vecs[:, V_C:V_C + 2 * KC].rearrange("p (w k) -> p k w", w=2),
                                 ACT.Silu).then_inc(c_ready, 1)
            sums_of_squares(x_in, pe_in, x_ready, (1, 2), 0)
            act.wait_ge(ctx_landed, 16)
            sums_of_squares(ctx_in, pe_in, x_ready, (2, 2), 2)
            split()
            for m in range(4):
                pairs = (2 * m, 2 * m + 1)
                act.wait_ge(gain_ready, 2 * (m + 1))
                norm_out(a_hi, modc(0, SHIFT_MIX), a32_mix, gain, pairs)
                norm_out(ac_hi, modc(0, SHIFT_MIX, 1), a32_mix, gain_ctx, pairs)
            split()
            D_.n += 1

            def log_gates(n):
                act.wait_ge(o_full, O_.at(1))
                if n > 0:
                    act.wait_ge(o_free, n)
                chained(nc.scalar.activation(gate_tmp, O[O_.n % 2][:, :], ACT.Abs))
                chained(nc.scalar.activation(gate_tmp, gate_tmp, ACT.Exp, scale=-1.0))
                nc.scalar.activation(gate_tmp, gate_tmp, ACT.Ln, bias=1.0).then_inc(log_ready, 1)
                O_.n += 1

            def tails(dst):
                for t in range(TT):
                    for d in range(2):
                        act.wait_ge(o_full, O_.at(1))
                        nc.scalar.activation(dst[:, t, d, :], O[O_.n % 2][:, :], ACT.Exp).then_inc(exp_ready, 1)
                        O_.n += 1

            def head_exps(hd):
                act.wait_ge(t_full, T_.at(1))
                T_.n += 1
                both_d = T[:, :].rearrange("p (d s) -> p d s", d=2)
                nc.scalar.activation(qd, both_d, ACT.Exp)
                nc.scalar.activation(ki, both_d, ACT.Exp, scale=-1.0).then_inc(exp_ready, 1)

            def y_out(k0):
                act.wait_ge(t_full, T_.at(1))
                nc.scalar.activation(a_hi[:, k0:k0 + 2, :], T[:, :].rearrange("p (k s) -> p k s", k=2),
                                     ACT.Copy).then_inc(y_hi, 1)
                T_.n += 1

            ad = Ada()
            T_.n = 2 + START_UNITS
            ad.slabs = 4 * START_UNITS
            for n, (what, n0, shared) in enumerate(MIX):
                for q in range(KC // KS):
                    split()
                    T_.n += ad.turned()
                    if n == 0:
                        log_gates(2 * q)
                        log_gates(2 * q + 1)
                    if q == 3:
                        tiles = 2 * TT if shared else TT
                        for t in range(tiles):
                            if what == "r":
                                tile_ends(t == tiles - 1)
                                nc.scalar.activation(r_tok[:, t, n0 - R_OFF:n0 - R_OFF + NW], A[(A_MIX[n] + t) % 4][:, :],
                                                     ACT.Sigmoid).then_inc(sig_ready, 1)
                            elif t < tiles - 1:
                                D_.n += 1
                    if n == 3 and q == 0:
                        tails(kc_tail)
                    if n == 3 and q == 1:
                        O_.n += HEADS
                    if n == 3 and q == 2:
                        tails(k_tail)
                    if n == 4 and q == 0:
                        T_.n += 4
                    if n >= 4:
                        if q == 0:
                            head_exps(n - 4)
                        if q == 1:
                            T_.n += 1
                            O_.n += 2
                        if q == 2:
                            O_.n += 4
                        if q == 3:
                            act.wait_ge(a_full, F.at(1))
                            F.n += 1
                            if n > 4:
                                act.wait_ge(a_free, A_MIX[n - 1] + 3)
                            for t in range(TT):
                                if t == 1:
                                    act.wait_ge(osq_ready, TT * (n - 4) + 1)
                                nc.scalar.activation(o_dump, A[(A_MIX[n] + 2) % 4][:, t * DV:(t + 1) * DV], ACT.Square,
                                                     accum_out=ssq[:, 4 + t:5 + t]).then_inc(osq_ready, 1)
                            root(rstd[:, 4:4 + TT])
                    ad.work(2 if shared else 1)

            for g in range(4):
                O_.n += 2
                y_out(8 + 2 * g)
            for j in range(4):
                y_out(2 * j)
            for m in range(4):
                for q in range(KC // KS):
                    split()
                    T_.n += ad.turned() + (q == 0)
                    ad.work(1)
                D_.n += 1
            T_.n += ad.turned()

            def ffn(layer):
                sums_of_squares(h, acc, h_ready, (2 * layer + 1, 2 * layer + 1), 0)
                act.wait_ge(gain_ready, 9 + 2 * layer)
                norm_out(a_hi, modc(layer, SHIFT_FFN), a32_ffn)

                def block_in():
                    for n in range(8):
                        split()
                        if layer == 0:
                            T_.n += ad.turned()
                            ad.work(ADA_FFN[n])
                        if n == 3:
                            for t in range(TT):
                                tile_ends(t == TT - 1)
                                nc.scalar.activation(sg[:, t, :], A[t][:, :], ACT.Silu).then_inc(sg_ready, 1)
                    D_.n += 1

                def hidden_hi():
                    for t, bank in enumerate((T, AD)):
                        act.wait_ge(t_full, T_.at(1))
                        nc.scalar.activation(hid_hi[:, :, t * P:(t + 1) * P],
                                             bank[:, :].rearrange("p (k s) -> p k s", k=KS), ACT.Copy).then_inc(hid_hi_ready, 1)
                        T_.n += 1

                block_in()
                hidden_hi()
                for i in loop(act, FB - 1, (S, 12), (W, 12), (D_, 6), (T_, 3 if layer == 0 else 2)):
                    block_in()
                    for m in range(4):
                        split()
                        D_.n += 1
                    hidden_hi()
                for m in range(4):
                    split()
                    D_.n += 1
                    T_.n += 1

            FREE.n = A_MIX[-1] + 3 + 8
            ffn(0)

            sums_of_squares(h, acc, h_ready, (2, 2), 0)
            act.wait_ge(gain_ready, 10)
            FREE.n += 4 * FB
            norm_out(a_hi, modc(1, SHIFT_MIX), a32_ffn)
            C = Tally()

            def conv_products(piece, b_col, first, last):
                for tap in range(first, last):
                    if tap == 0:
                        act.wait_ge(t_free, T_.at())
                    if C.n > 0 or C.it is not None:
                        if tap == 0 or tap >= 4:
                            act.wait_ge(prod_added, C.at(0 if tap == 0 else -3))
                    w = w_dw[:, piece, tap:tap + 1].rearrange("p a b -> p (a b)")
                    dst = prod[:, tap % 4:tap % 4 + 1, :]
                    src = uT[:, piece, tap:tap + SEQ]
                    if tap == 0:
                        nc.scalar.activation(dst, src, ACT.Identity, scale=w, bias=b_col).then_inc(prod_ready, 1)
                    else:
                        nc.scalar.activation(dst, src, ACT.Copy, scale=w).then_inc(prod_ready, 1)
                    C.n += 1
                if last == CONV_W:
                    act.wait_ge(prod_added, C.at())
                    nc.scalar.activation(conv_v[:, piece, :], pool_acc[:, None, :], ACT.Copy).then_inc(piece_done, 1)

            def pw1_block(piece, b_col):
                taps = 0
                for n in range(8):
                    split()
                    T_.n += ad.turned()
                    if piece is not None and n in (1, 2):
                        T_.n += 1
                    if piece is not None and n >= 2:
                        more = 6 if n == 2 else 5
                        conv_products(piece, b_col, taps, taps + more)
                        taps += more
                    if n == 3:
                        D_.n += 1
                    if n == 7:
                        for t in range(TT):
                            tile_ends(t == TT - 1)
                            nc.scalar.activation(sg[:, t, :], A[2 + t][:, :], ACT.Sigmoid).then_inc(sg_ready, 1)
                    ad.work(ADA_PW1[n])

            ad.slabs = 4 * 34
            pw1_block(None, None)
            for i in loop(act, 3, (S, 8), (W, 8), (D_, 2), (T_, 4), (C, CONV_W)):
                pw1_block(bass.ds(i * KS + (KS - 1), 1), vecs[:, bass.ds(i * KS + (V_BDW + KS - 1), 1)])
            T_.n += 2
            conv_products(slice(KC - 1, KC), vecs[:, V_LNG - 1:V_LNG], 0, CONV_W)
            for g in range(4):
                act.wait_ge(xc_ready, g + 1)
                nc.scalar.activation(sq[:, 4 * g:4 * g + 4, :], conv_v[:, 4 * g:4 * g + 4, :], ACT.Square).then_inc(sq_ready, 1)
            root(rstd_bc)
            for j in range(KC // 2):
                act.wait_ge(yn_ready, j // 2 + 1)
                if j >= 2:
                    act.wait_ge(ln_lo, j - 1)
                for e in range(2):
                    k = 2 * j + e
                    chained(nc.scalar.activation(a32_ffn[:, j % 2, e, :], conv_v[:, k, :], ACT.Silu,
                                                 bias=vecs[:, V_LNB + k:V_LNB + k + 1], scale=vecs[:, V_LNG + k:V_LNG + k + 1]))
                nc.scalar.activation(a_hi[:, 2 * j:2 * j + 2, :], a32_ffn[:, j % 2, :, :], ACT.Copy).then_inc(ln_hi, 1)
            for m in range(4):
                for q in range(KC // KS):
                    split()
                    T_.n += ad.turned() + (q == 0)
                    ad.work(1 + (q + 1) % 2)
                D_.n += 1
            T_.n += ad.turned()
            FREE.n = FREE.n + 16 + 8
            ffn(1)
            sums_of_squares(h, acc, h_ready, (4, 4), 0)

        @block.vector
        def _(dve):
            S, W, D_, F, T_, O_, FREE, OW = Tally(), Tally(), Tally(), Tally(), Tally(), Tally(), Tally(), Tally()
            G, SIG, SG, H, X = Tally(), Tally(), Tally(), Tally(), Tally()
            step, norms, ssqs = [0], [0], [0]
            W.n = -1

            def split():
                W.n += 1
                if S.n == SLABS:
                    return
                dve.wait_ge(hi_ready, S.at(1))
                nc.vector.tensor_tensor(w_lo[:, S.n % 2, :], w_raw[:, S.n % 4, :], w_hi[:, S.n % 2, :].bitcast(F32),
                                        ALU.subtract).then_inc(lo_ready, 1)
                S.n += 1

            def tile_ends(last):
                if last:
                    dve.wait_ge(w_used, W.at())
                else:
                    dve.wait_ge(tile_done, D_.at(1))
                    D_.n += 1

            def chained(ins):
                step[0] += 1
                ins.then_inc(dve_step, 1)
                dve.wait_ge(dve_step, step[0])

            def t_whole():
                dve.wait_ge(t_full, T_.at(1))
                T_.n += 1

            def o_whole():
                OW.n += 1
                dve.wait_ge(o_full, OW.at())
                O_.n += 1
                return O[(O_.n - 1) % 2]

            def freed():
                FREE.n += 1
                return A[(FREE.n - 1) % 4]

            ad = Ada()

            def ada_add(offset=None):
                t_whole()
                dst = mod[:, (G.n - 1) * 4:G.n * 4, :] if offset is None else mod[:, bass.ds(offset, 4), :]
                if G.it is None and not summed_by_dve(G.n - 1) or G.it is not None and not summed_by_dve(G.n):
                    turned = T[:, 0:8].rearrange("p (k w) -> p k w", w=2)
                else:
                    dst, turned = dst[:, :, 0:1], T[:, 0:4].rearrange("p (k w) -> p k w", w=1)
                nc.vector.tensor_tensor(dst, dst, turned, ALU.add).then_inc(t_free, 1)

            def ada_copy(sem_=ada_used, value=None):
                G.n += 1
                if value is None:
                    value = USED.at(4)
                    USED.n += 4
                    U.n += 4
                dve.wait_ge(sem_, value)
                nc.vector.tensor_copy(ada_rows[:, :], AD[:, :]).then_inc(rows_copied, 1)

            USED = Tally()
            U, V = Tally(), Tally()

            def ada_sum(slabs):
                for _ in range(slabs):
                    q = U.n % 4
                    dve.wait_ge(ada_landed[U.n % 2], U.landed(2))
                    for k in range(KS):
                        w, cc = ada_raw[:, U.n % 2, k * NW:(k + 1) * NW], c_pad[:, KS * q + k, 0:1]
                        if q == 0 and k == 0:
                            nc.vector.tensor_scalar(ada_rows[:, :], w, cc, None, ALU.mult).then_inc(ada_summed, 1)
                        else:
                            dve.wait_ge(ada_summed, V.at())
                            nc.vector.scalar_tensor_tensor(out=ada_rows[:, :], in0=w, scalar=cc, in1=ada_rows[:, :],
                                                           op0=ALU.mult, op1=ALU.add).then_inc(ada_summed, 1)
                        V.n += 1
                    U.n += 1
                    if q == 3:
                        G.n += 1

            def inverse_root(v):
                nc.vector.reciprocal(v, v).then_inc(recip_ready, 1)
                R.n += 1
                dve.wait_ge(root_ready, R.n)

            R = Tally()

            def inverse_rms(slot, n, width):
                chained(nc.vector.tensor_scalar(rstd[:, slot:slot + n], ssq[:, slot:slot + n], 1.0 / width, EPS, ALU.mult, ALU.add))
                inverse_root(rstd[:, slot:slot + n])

            def normed(dst, src, slot):
                ssqs[0] += TT
                dve.wait_ge(ssq_ready, ssqs[0])
                inverse_rms(slot, TT, D)
                for t in range(TT):
                    nc.vector.tensor_scalar(dst[:, t, :], src[:, t, :], rstd[:, slot + t:slot + t + 1], None,
                                            ALU.mult).then_inc(hn_ready, 1)

            def set_gain(layer, what, g0, which=0, k0=0, k1=KC):
                dst = gain_ctx if which else gain
                nc.vector.scalar_tensor_tensor(out=dst[:, k0:k1], in0=modc(layer, what, which)[:, k0:k1], scalar=1.0,
                                               in1=vecs[:, g0 + k0:g0 + k1], op0=ALU.add, op1=ALU.mult).then_inc(gain_ready, 1)
                norms[0] += 1
                dve.wait_ge(gain_ready, norms[0])

            def norm_out(hi, lo, add, a32, g=gain, pairs=range(KC // 2)):
                def lo_part(j):
                    X.n += 1
                    dve.wait_ge(hi_done, X.n)
                    nc.vector.tensor_tensor(lo[:, 2 * j:2 * j + 2, :], a32[:, j % 2, :, :], hi[:, 2 * j:2 * j + 2, :].bitcast(F32),
                                            ALU.subtract).then_inc(a_free, 1)

                for j in pairs:
                    k = 2 * j
                    dve.wait_ge(a_full, F.at(1))
                    F.n += 1
                    if FREE.n >= 2:
                        dve.wait_ge(a_free, FREE.n - 1)
                    nc.vector.tensor_scalar(a32[:, j % 2, 0, :], freed()[:, 0:SEQ], g[:, k:k + 1], add[:, k:k + 1],
                                            ALU.mult, ALU.add).then_inc(a32_even, 1)
                    if j > pairs[0]:
                        lo_part(j - 1)
                lo_part(pairs[-1])

            def diagonal(layer, what, m, last=False):
                for k in range(KS):
                    ins = nc.vector.tensor_scalar(diag[:, k * P:(k + 1) * P], ident, modc(layer, what)[:, m * KS + k:m * KS + k + 1],
                                                  None, ALU.mult)
                ins.then_inc(diag_ready, 1)

            def gate_quarter(layer, what, m):
                t_whole()
                nc.vector.tensor_copy(gate_bc[:, m * NW:(m + 1) * NW], T[:, :]).then_inc(t_free, 1)
                if m < 3:
                    diagonal(layer, what, m + 1)

            def residual(t, m, last):
                cols = slice(m * NW, (m + 1) * NW)
                tile_ends(t == TT - 1)
                nc.vector.tensor_tensor(sg[:, t, :], freed()[:, :], gate_bc[:, cols], ALU.mult).then_inc(a_free, 1)
                dve.wait_ge(a_free, FREE.at())
                ins = nc.vector.tensor_tensor(h[:, t, cols], h[:, t, cols], sg[:, t, :], ALU.add)
                if last:
                    ins.then_inc(h_ready, 1)

            nc.vector.memset(dw_stage[0:32, :], 0.0).then_inc(cleared, 1)
            nc.vector.memset(w2[0:2 * RANK + 1, :, :], 0.0).then_inc(w2_cleared, 1)
            nc.vector.memset(ones[:, :], 1.0)
            nc.vector.memset(z_aug[0:2 * RANK + 1, :], 1.0)
            nc.vector.memset(c_pad[:, :, :], 0.0).then_inc(cleared, 1)
            t_whole()
            nc.vector.tensor_copy(vecs[:, :], T[:, 0:V_END]).then_inc(t_free, 1)
            dve.wait_ge(t_free, 1)
            for w in range(2):
                for layer, v0 in ((0, V_ADAB0), (1, V_ADAB1)):
                    ins = nc.vector.tensor_copy(mod[:, layer * 6 * KC:(layer + 1) * 6 * KC, w], vecs[:, v0:v0 + 6 * KC])
            ins.then_inc(cleared, 1)
            t_whole()
            nc.vector.tensor_copy(w_dw[:, :, :], T[:, :].rearrange("p (k t) -> p k t", k=KC)).then_inc(t_free, 1)
            dve.wait_ge(x_landed, 32)
            for t in range(TT):
                nc.vector.tensor_tensor(x_in[:, t, :], x_in[:, t, :], pe_in[:, t, :], ALU.add).then_inc(x_ready, 1)
            normed(x_in, x_in, 0)
            normed(ctx_in, ctx_in, 2)
            for n, u in enumerate(START_ORDER):
                ada_copy(start_used, 4 * (n + 1))
                ada_add(4 * u)
                if n == 0:
                    split()
                if n % 2 == 1:
                    dve.wait_ge(t_free, T_.at())
                    k0, pairs = (n // 2) * KS, (n - 1, n)
                    set_gain(0, SCALE_MIX, V_MIXG, 0, k0, k0 + KS)
                    set_gain(0, SCALE_MIX, V_MIXG, 1, k0, k0 + KS)
                    norm_out(a_hi, a_lo, modc(0, SHIFT_MIX), a32_mix, gain, pairs)
                    norm_out(ac_hi, ac_lo, modc(0, SHIFT_MIX, 1), a32_mix, gain_ctx, pairs)
            split()
            dve.wait_ge(c_ready, 1)
            for n in range(2):
                if n == 0:
                    dve.wait_ge(tile_done, D_.at(1))
                    D_.n += 1
                else:
                    dve.wait_ge(w_used, 1)
                nc.vector.tensor_copy(z_aug[0:2 * RANK, n * SEQ:(n + 1) * SEQ], freed()[0:2 * RANK, 0:SEQ]).then_inc(a_free, 1)

            E = Tally()

            def log_gate(n):
                t, d = n // 2, n % 2
                dst = (g_tok[:, t, d, :] if t < TT else gc_tok[:, t - TT, d, :])
                bank = o_whole()
                dve.wait_ge(log_ready, n + 1)
                nc.vector.scalar_tensor_tensor(out=dst, in0=bank[:, :], scalar=0.0, in1=gate_tmp, op0=ALU.min,
                                               op1=ALU.subtract).then_inc(o_free, 1)

            def tails(dst, keys):
                for t in range(TT):
                    for d in range(2):
                        o_whole()
                        E.n += 1
                        dve.wait_ge(exp_ready, E.n)
                        nc.vector.tensor_tensor(dst[:, t, d, :], dst[:, t, d, :], keys[:, t, :], ALU.mult).then_inc(o_free, 1)

            def head_decays(hd):
                t_whole()
                E.n += 1
                dve.wait_ge(exp_ready, E.n)
                nc.vector.tensor_copy(dec[:, 0, :], qd[:, 0, :].rearrange("p (c s) -> p c s", s=CHUNK)[:, :, CHUNK - 1])
                chained(nc.vector.tensor_copy(dec[:, 1, :], qd[:, 1, :].rearrange("p (c s) -> p c s", s=CHUNK)[:, :, 0]))
                for d in range(2):
                    nc.vector.tensor_tensor(ki[:, d, :], ki[:, d, :], kT[:, hd, :], ALU.mult)
                    ins = nc.vector.tensor_tensor(qd[:, d, :], qd[:, d, :], qT[:, hd, :], ALU.mult)
                ins.then_inc(t_free, 1)

            def head_mask(hd):
                t_whole()
                for d in range(2):
                    for t in range(TT):
                        n = (d * TT + t) * P
                        ins = nc.vector.copy_predicated(att[:, d, t, :], mat(M_INC_B if d else M_INC_F).bitcast(U32),
                                                        T[:, n:n + P])
                ins.then_inc(t_free, 1)

            def head_state(hd, m):
                for d in range(2):
                    bank = o_whole()
                    dve.wait_ge(o_free, O_.at(-2) if m > 0 else O_.at(-1))
                    ch = 3 - m if d else m
                    old = ctx_state[:, hd, d, :] if m == 0 else states[:, d, m - 1, :]
                    ins = nc.vector.scalar_tensor_tensor(out=states[:, d, m, :], in0=old, scalar=dec[:, d, ch:ch + 1],
                                                         in1=bank[:, 0:DV], op0=ALU.mult, op1=ALU.add)
                    ins.then_inc(o_free, 1)

            def head_gate(hd):
                dve.wait_ge(a_full, F.at(1))
                F.n += 1
                dve.wait_ge(osq_ready, TT * (hd + 1))
                inverse_rms(4, TT, DV)
                bank = freed()
                for t in range(TT):
                    ins = nc.vector.scalar_tensor_tensor(out=o_tmp[:, t, :], in0=bank[:, t * DV:(t + 1) * DV],
                                                         scalar=rstd[:, 4 + t:5 + t], in1=gla_g[:, :], op0=ALU.mult, op1=ALU.mult)
                ins.then_inc(a_free, 1)
                dve.wait_ge(a_free, FREE.at())
                for t in range(TT):
                    dst = r_tok[:, t, hd * DV:(hd + 1) * DV]
                    nc.vector.tensor_tensor(dst, dst, o_tmp[:, t, :], ALU.mult).then_inc(gated, 1)

            ad.slabs = 4 * START_UNITS
            for n, (what, n0, shared) in enumerate(MIX):
                for q in range(KC // KS):
                    split()
                    if ad.turned():
                        ada_add()
                    if n == 0:
                        log_gate(2 * q)
                        log_gate(2 * q + 1)
                    if q == 3:
                        tiles = 2 * TT if shared else TT
                        assert FREE.n == A_MIX[n]
                        for t in range(tiles):
                            tile_ends(t == tiles - 1)
                            bank = freed()
                            if what == "k":
                                ins = nc.vector.tensor_copy((k_tok if t < TT else kc_tok)[:, t % TT, :], bank[:, :])
                            elif what == "v":
                                ins = nc.vector.tensor_copy((v_tok if t < TT else vc_tok)[:, t % TT, n0 - V_OFF:n0 - V_OFF + NW], bank[:, :])
                            elif what == "q":
                                ins = nc.vector.tensor_scalar(q_tok[:, t, :], bank[:, :], DK ** -0.5, None, ALU.mult)
                            elif what == "r":
                                SIG.n += 1
                                dve.wait_ge(sig_ready, SIG.n)
                                dst = r_tok[:, t, n0 - R_OFF:n0 - R_OFF + NW]
                                ins = nc.vector.tensor_tensor(dst, dst, bank[:, :], ALU.mult)
                            else:
                                ins = nc.vector.tensor_copy(f_tok[:, t, n0 - F_OFF:n0 - F_OFF + NW], bank[:, :])
                            ins.then_inc(a_free, 1)
                    if n == 0 and q == 3:
                        dve.wait_ge(o_free, 8)
                        nc.vector.memset(att, 0.0)
                    if n == 3 and q == 0:
                        tails(kc_tail, kc_tok)
                    if n == 3 and q == 1:
                        for hd in range(HEADS):
                            nc.vector.tensor_copy(ctx_state[:, hd, :, :].rearrange("p d v -> p (d v)"),
                                                  o_whole()[:, :]).then_inc(o_free, 1)
                    if n == 3 and q == 2:
                        tails(k_tail, k_tok)
                    if n == 4 and q == 0:
                        for dst in (qT, kT):
                            for t in range(TT):
                                t_whole()
                                nc.vector.tensor_copy(dst[:, :, t * P:(t + 1) * P],
                                                      T[:, :].rearrange("p (k s) -> p k s", k=HEADS)).then_inc(t_free, 1)
                    if n >= 4:
                        hd = n - 4
                        if q == 0:
                            head_decays(hd)
                        if q == 1:
                            head_mask(hd)
                            head_state(hd, 0)
                        if q == 2:
                            head_state(hd, 1)
                            head_state(hd, 2)
                        if q == 3:
                            head_gate(hd)
                    if shared:
                        ada_sum(2)
                        ad.work(2)
                    elif ad.work(1):
                        ada_copy()

            Y = Tally()

            def y_lo(k0):
                t_whole()
                Y.n += 1
                dve.wait_ge(y_hi, Y.n)
                nc.vector.tensor_tensor(a_lo[:, k0:k0 + 2, :], T[:, :].rearrange("p (k s) -> p k s", k=2),
                                        a_hi[:, k0:k0 + 2, :].bitcast(F32), ALU.subtract).then_inc(t_free, 1)

            for g in range(4):
                for dc in range(2):
                    nc.vector.tensor_copy(fn_cs[:, g % 2, dc, :], o_whole()[:, :]).then_inc(o_free, 1)
                y_lo(8 + 2 * g)
            for j in range(4):
                y_lo(2 * j)
            diagonal(0, GATE_MIX, 0)
            for m in range(4):
                for q in range(KC // KS):
                    split()
                    if ad.turned():
                        ada_add()
                    if q == 0:
                        gate_quarter(0, GATE_MIX, m)
                    if m == 0 and q == 3:
                        dve.wait_ge(h_landed, 32)
                        for t in range(TT):
                            ins = nc.vector.tensor_tensor(h[:, t, :], h[:, t, :], pe_out[:, t, :], ALU.add)
                        chained(ins)
                        dve.wait_ge(t_free, T_.at())
                    if q == 3:
                        for t in range(TT):
                            residual(t, m, m == 3 and t == TT - 1)
                    if ad.work(1):
                        ada_copy()
            if ad.turned():
                ada_add()

            def ffn(layer):
                dve.wait_ge(h_ready, 2 * layer + 1)
                dve.wait_ge(t_free, T_.at())
                normed(acc, h, 0)
                set_gain(layer, SCALE_FFN, V_FFNG + layer * KC)
                norm_out(a_hi, a_lo, modc(layer, SHIFT_FFN), a32_ffn)
                nc.vector.memset(acc, 0.0)

                def block_in(offset):
                    for n in range(8):
                        split()
                        if layer == 0 and ad.turned():
                            ada_add(offset)
                        if n == 3:
                            D_.n += 1
                        if n == 7:
                            for t in range(TT):
                                dve.wait_ge(sg_ready, SG.at(1))
                                SG.n += 1
                                tile_ends(t == TT - 1)
                                ins = nc.vector.tensor_tensor(hid_tok[:, t, :], A[2 + t][:, :], sg[:, t, :], ALU.mult)
                            ins.then_inc(a_free, 4)
                            FREE.n += 4
                        if layer == 0:
                            ada_sum(ADA_FFN[n])
                            ad.work(ADA_FFN[n])

                def hidden_lo():
                    for t, bank in enumerate((T, AD)):
                        t_whole()
                        dve.wait_ge(hid_hi_ready, H.at(1))
                        H.n += 1
                        nc.vector.tensor_tensor(hid_lo[:, :, t * P:(t + 1) * P], bank[:, :].rearrange("p (k s) -> p k s", k=KS),
                                                hid_hi[:, :, t * P:(t + 1) * P].bitcast(F32), ALU.subtract).then_inc(t_free, 1)

                def o_ends(t):
                    tile_ends(t == TT - 1)
                    O_.n += 1
                    return O[t]

                block_in(None)
                hidden_lo()
                steps = [(S, 12), (W, 12), (D_, 6), (SG, 2), (FREE, 4), (H, 2), (O_, 8)]
                steps += [(T_, 3), (U, 4), (V, 16), (G, 1)] if layer == 0 else [(T_, 2)]
                for i in loop(dve, FB - 1, *steps):
                    block_in(i * 4 + 24 * 4)
                    for m in range(4):
                        split()
                        for t in range(TT):
                            cols = slice(m * NW, (m + 1) * NW)
                            bank = o_ends(t)
                            nc.vector.tensor_tensor(acc[:, t, cols], acc[:, t, cols], bank[:, :], ALU.add).then_inc(o_free, 1)
                    hidden_lo()
                diagonal(layer, GATE_FFN, 0)
                for m in range(4):
                    split()
                    for t in range(TT):
                        cols = slice(m * NW, (m + 1) * NW)
                        bank = o_ends(t)
                        nc.vector.tensor_tensor(acc[:, t, cols], acc[:, t, cols], bank[:, :], ALU.add).then_inc(o_free, 1)
                        dve.wait_ge(o_free, O_.at())
                        if t == 0:
                            gate_quarter(layer, GATE_FFN, m)
                            dve.wait_ge(t_free, T_.at())
                        chained(nc.vector.tensor_tensor(acc[:, t, cols], acc[:, t, cols], gate_bc[:, cols], ALU.mult))
                        ins = nc.vector.tensor_tensor(h[:, t, cols], h[:, t, cols], acc[:, t, cols], ALU.add)
                        if m == 3 and t == TT - 1:
                            ins.then_inc(h_ready, 1)

            ffn(0)

            dve.wait_ge(t_free, T_.at())
            normed(acc, h, 0)
            set_gain(1, SCALE_MIX, V_MIXG + KC)
            nc.vector.memset(uT[:, :, 0:HALO], 0.0)
            nc.vector.memset(uT[:, :, HALO + SEQ:], 0.0)
            norm_out(a_hi, a_lo, modc(1, SHIFT_MIX), a32_ffn)
            C = Tally()

            def taps(piece, b_col, first, last):
                for n in range(first, last):
                    tap, m = n // (KS - 1), n % (KS - 1)
                    p = piece(m)
                    w = w_dw[:, p, tap:tap + 1].rearrange("p a b -> p (a b)")
                    dst, src = conv_v[:, p, :], uT[:, p, tap:tap + SEQ]
                    if n == 0:
                        dve.wait_ge(t_free, T_.at())
                    if tap == 0:
                        nc.vector.tensor_scalar(dst, src, w, b_col(m), ALU.mult, ALU.add).then_inc(conv_dve, 1)
                    else:
                        dve.wait_ge(conv_dve, C.at(2 - KS))
                        nc.vector.scalar_tensor_tensor(out=dst, in0=src, scalar=w, in1=dst, op0=ALU.mult,
                                                       op1=ALU.add).then_inc(conv_dve, 1)
                    C.n += 1

            def u_tile(dst_pieces, t):
                t_whole()
                nc.vector.tensor_copy(uT[:, dst_pieces, HALO + t * P:HALO + (t + 1) * P],
                                      T[:, :].rearrange("p (k s) -> p k s", k=KS)).then_inc(t_free, 1)

            def pw1_block(offsets, before, piece, b_col):
                done = 0
                for n in range(8):
                    split()
                    if ad.turned():
                        ada_add(offsets[0 if n < 6 else 1])
                    if before is not None and n in (1, 2):
                        u_tile(before, n - 1)
                    if before is not None and n >= 2:
                        more = 16 if n < 5 else 15
                        taps(piece, b_col, done, done + more)
                        done += more
                    if n == 3:
                        D_.n += 1
                    if n == 7:
                        for t in range(TT):
                            dve.wait_ge(sg_ready, SG.at(1))
                            SG.n += 1
                            tile_ends(t == TT - 1)
                            ins = nc.vector.tensor_tensor(hid_tok[:, t, :], A[t][:, :], sg[:, t, :], ALU.mult)
                        ins.then_inc(a_free, 4)
                        FREE.n += 4
                    if ad.work(ADA_PW1[n]):
                        ada_copy()

            assert ad.slabs % 4 == 0
            pw1_block((None, None), None, None, None)
            for i in loop(dve, 3, (S, 8), (W, 8), (D_, 2), (T_, 4), (SG, 2), (FREE, 4), (USED, 8), (U, 8), (G, 2),
                          (C, CONV_W * (KS - 1))):
                pw1_block((i * 8 + 36 * 4, i * 8 + 37 * 4), bass.ds(i * KS, KS),
                          lambda m: bass.ds(i * KS + m, 1), lambda m: vecs[:, bass.ds(i * KS + (V_BDW + m), 1)])
            for t in range(TT):
                u_tile(slice(KC - KS, KC), t)
            taps(lambda m: slice(KC - KS + m, KC - KS + m + 1),
                 lambda m: vecs[:, V_BDW + KC - KS + m:V_BDW + KC - KS + m + 1], 0, CONV_W * (KS - 1))

            def over_channels(v):
                return v[:, None, :].to_broadcast([P, KS, SEQ])

            bank = o_whole()
            nc.vector.tensor_scalar(mean_bc, bank[:, 0:SEQ], 1.0 / D, None, ALU.mult).then_inc(o_free, 1)
            dve.wait_ge(o_free, O_.at())
            for g in range(4):
                v = conv_v[:, KS * g:KS * (g + 1), :]
                nc.vector.tensor_tensor(v, v, over_channels(mean_bc), ALU.subtract).then_inc(xc_ready, 1)
            bank = o_whole()
            nc.vector.tensor_scalar(rstd_bc, bank[:, 0:SEQ], 1.0 / D, EPS, ALU.mult, ALU.add).then_inc(o_free, 1)
            dve.wait_ge(o_free, O_.at())
            inverse_root(rstd_bc)
            for g in range(4):
                v = conv_v[:, KS * g:KS * (g + 1), :]
                nc.vector.tensor_tensor(v, v, over_channels(rstd_bc), ALU.mult).then_inc(yn_ready, 1)
            for j in range(KC // 2):
                dve.wait_ge(ln_hi, j + 1)
                nc.vector.tensor_tensor(a_lo[:, 2 * j:2 * j + 2, :], a32_ffn[:, j % 2, :, :],
                                        a_hi[:, 2 * j:2 * j + 2, :].bitcast(F32), ALU.subtract).then_inc(ln_lo, 1)
            diagonal(1, GATE_MIX, 0)
            for m in range(4):
                for q in range(KC // KS):
                    split()
                    if ad.turned():
                        ada_add()
                    if q == 0:
                        gate_quarter(1, GATE_MIX, m)
                        dve.wait_ge(t_free, T_.at())
                    if q == 3:
                        for t in range(TT):
                            residual(t, m, m == 3 and t == TT - 1)
                    if ad.work(1 + (q + 1) % 2):
                        ada_copy()
            if ad.turned():
                ada_add()
            ffn(1)

            ssqs[0] += TT
            dve.wait_ge(ssq_ready, ssqs[0])
            inverse_rms(0, TT, D)
            dve.wait_ge(fin_landed, 16)
            for t in range(TT):
                chained(nc.vector.tensor_scalar(h[:, t, :], h[:, t, :], rstd[:, t:t + 1], None, ALU.mult))
                nc.vector.tensor_tensor(h[:, t, :], h[:, t, :], fin_g, ALU.mult).then_inc(result_ready, 1)


_INS = ['x', 'c', 'ctx', 'c_ctx', 'ada_w', 'ada_b', 'norm_mix_g', 'norm_ffn_g', 'ffn_w_in', 'ffn_w_out', 'gm_w_in',
        'gla_gate_w_fwd', 'gla_gate_b_fwd', 'gla_gate_w_bwd', 'gla_gate_b_bwd', 'gla_norm_g', 'gm_w_out', 'cv_w_pw1',
        'cv_b_pw1', 'cv_w_dw', 'cv_b_dw', 'cv_ln_g', 'cv_ln_b', 'cv_w_pw2', 'cv_b_pw2', 'final_norm_g']
_OUTS = [((1, SEQ, D), 'float32')]


def _constants():
    import numpy as np
    grid_w = 64
    r = np.repeat(np.arange(SEQ // grid_w, dtype=np.float32), grid_w)
    col = np.tile(np.arange(grid_w, dtype=np.float32), SEQ // grid_w)
    nq = D // 4
    omega = (1.0 / (np.float32(10000.0) ** (np.arange(nq, dtype=np.float32) / np.float32(nq)))).astype(np.float32)
    ar, ac = r[:, None] * omega[None, :], col[:, None] * omega[None, :]
    pos = np.concatenate([np.sin(ar), np.cos(ar), np.sin(ac), np.cos(ac)], axis=-1).astype(np.float32)

    j, t = np.arange(P)[:, None], np.arange(P)[None, :]
    near = j // CHUNK == t // CHUNK
    norm = 1.0 / 16.0
    mats = [j == t, norm * (near & (j <= t)), norm * (near & (j >= t)), norm * (near & (j > t)),
            norm * (near & (j < t)), norm * (j > t), norm * (j < t), norm * np.ones((P, P))]
    pick = np.stack([np.arange(P) % 32 == 0, np.arange(P) % 32 == 1], axis=1)
    matrices = np.concatenate([np.asarray(m, np.float32) for m in mats + [pick]], axis=1)

    n = np.arange(SEQ)
    angle = 2 * np.pi * (np.outer(n, n) % SEQ) / SEQ
    cos, sin = np.cos(angle) / 16.0, np.sin(angle) / 16.0
    dft = np.concatenate([cos, sin, -sin], axis=1).astype(np.float32)
    return {'pos_embed': pos, 'matrices': np.ascontiguousarray(matrices), 'dft': dft}


def kernel(**inputs):
    import numpy as _np
    import concourse.bacc as _bacc
    from concourse import mybir as _mybir
    from concourse.bass_utils import run_bass_kernel_spmd as _run

    nc = _bacc.Bacc("TRN2", target_bir_lowering=False, num_devices=1)
    arrays, args = {}, []
    given = {name: _np.ascontiguousarray(inputs[name]) for name in _INS}
    for name, a in list(given.items()) + list(_constants().items()):
        arrays[f"in_{name}_dram"] = a
        args.append(nc.dram_tensor(f"in_{name}_dram", a.shape, _mybir.dt.from_np(a.dtype), kind="ExternalInput").ap())
    for i, (shape, dtype) in enumerate(_OUTS):
        dt = _mybir.dt.from_np(_np.dtype(dtype))
        args.append(nc.dram_tensor(f"out_{i}_dram", shape, dt, kind="ExternalOutput").ap())
    program(nc, *args)
    r = _run(nc, [arrays], core_ids=[0])
    return r.results[0]["out_0_dram"]
```

```python
from contextlib import ExitStack

import concourse.bass as bass
from concourse import mybir

F32 = mybir.dt.float32
F32R = mybir.dt.float32r
U32 = mybir.dt.uint32
ALU = mybir.AluOpType
ACT = mybir.ActivationFunctionType

P = 128
D = 2048
KC = D // P
SEQ = 256
TT = SEQ // P
HEADS, DK, DV, CHUNK, RANK = 4, 128, 256, 64, 16
FN_W = 256
NW = 512
KS = 4
Q_OFF, K_OFF, V_OFF, R_OFF, Z_OFF, F_OFF = 0, 512, 1024, 2048, 3072, 3104
IN_W = 4128
D_FF = 5632
FB = D_FF // NW
CONV_W = 31
HALO = CONV_W // 2
EPS = 1e-6

SHIFT_MIX, SCALE_MIX, GATE_MIX, SHIFT_FFN, SCALE_FFN, GATE_FFN = range(6)
UNITS = 6 * D // NW

V_ADAB0, V_C, V_ADAB1, V_MIXG, V_FFNG, V_BDW, V_LNG, V_LNB, V_END = 0, 96, 128, 224, 256, 288, 304, 320, 336

(M_IDENT, M_INC_F, M_INC_B, M_AFTER, M_BEFORE, M_AFTER_ALL, M_BEFORE_ALL, M_ALL) = [P * n for n in range(8)]
M_PICK = P * 8
M_END = M_PICK + 2


class Ada:

    def __init__(self):
        self.slabs, self.pending = 0, 0

    def turned(self):
        was, self.pending = self.pending, 0
        return was

    def work(self, n):
        done = (self.slabs + n) // 4 - self.slabs // 4
        self.slabs += n
        self.pending |= done
        return done


class Tally:

    def __init__(self):
        self.n, self.per, self.it = 0, 0, None

    def at(self, more=0):
        return self.n + more if self.it is None else self.it * self.per + (self.n + more)

    def landed(self, ring):
        v = 16 * (self.n // ring + 1)
        return v if self.it is None else self.it * (16 * self.per // ring) + v


def loop(eng, count, *tallies_and_steps):
    with eng.Fori(0, count) as it:
        start = []
        for tally, per in tallies_and_steps:
            start.append(tally.n)
            tally.it, tally.per = it, per
        yield it
        for (tally, per), n in zip(tallies_and_steps, start):
            assert tally.n == n + per, (tally.n, n, per)
    for (tally, per), n in zip(tallies_and_steps, start):
        tally.n, tally.it = n + count * per, None


def program(nc, x, c, ctx, c_ctx, ada_w, ada_b, norm_mix_g, norm_ffn_g, ffn_w_in, ffn_w_out, gm_w_in,
            gate_w_f, gate_b_f, gate_w_b, gate_b_b, gla_norm_g, gm_w_out, cv_w_pw1, cv_b_pw1, cv_w_dw,
            cv_b_dw, cv_ln_g, cv_ln_b, cv_w_pw2, cv_b_pw2, final_norm_g, pos_embed, matrices, dft, out):
    with ExitStack() as stack:
        def sb(name, shape, dt=F32, on=stack):
            return on.enter_context(nc.sbuf_tensor(name, shape, dt))

        def sem(name):
            return stack.enter_context(nc.semaphore(name))

        w_raw = sb("w_raw", [P, 4, KS * NW])
        w_hi = sb("w_hi", [P, 2, KS * NW], F32R)
        w_lo = sb("w_lo", [P, 2, KS * NW], F32R)
        ada_raw = sb("ada_raw", [P, 2, KS * NW])
        a_hi = sb("a_hi", [P, KC, SEQ], F32R)
        a_lo = sb("a_lo", [P, KC, SEQ], F32R)
        mats = sb("mats", [P, M_END])
        ones = sb("ones", [P, P])
        mod = sb("mod", [P, 2 * 6 * KC, 2])
        vecs = sb("vecs", [P, V_END])
        w_dw = sb("w_dw", [P, KC, 32])
        c_pad = sb("c_pad", [P, KC, 32])
        ada_rows = sb("ada_rows", [P, NW])
        ssq = sb("ssq", [P, 16])
        rstd = sb("rstd", [P, 8])
        gain = sb("gain", [P, KC])
        gain_ctx = sb("gain_ctx", [P, KC])
        gla_g = sb("gla_g", [P, DV])
        arena0 = sb("arena0", [P, 20 * 256])
        with ExitStack() as early:
            ac_hi = sb("ac_hi", [P, KC, SEQ], F32R, early)
            ac_lo = sb("ac_lo", [P, KC, SEQ], F32R, early)
        with ExitStack() as late:
            hid_hi = sb("hid_hi", [P, KS, SEQ], F32R, late)
            hid_lo = sb("hid_lo", [P, KS, SEQ], F32R, late)
        arena1 = sb("arena1", [P, 32 * 256])
        arena2 = sb("arena2", [P, 28 * 256])

        def part(arena, kib, *shape):
            n = 1
            for d in shape:
                n *= d
            flat = arena[:, int(kib * 256):int(kib * 256) + n]
            if len(shape) == 1:
                return flat
            names = "abcd"[:len(shape)]
            return flat.rearrange(f"p ({' '.join(names)}) -> p {' '.join(names)}",
                                  **{k: v for k, v in zip(names[1:], shape[1:])})

        x_in = part(arena0, 0, TT, D)
        ctx_in = part(arena2, 0, TT, D)
        pe_in = part(arena1, 0, TT, D)
        dw_stage = part(arena1, 16, D)
        vec_stage = part(arena1, 24, 3, P)
        a32_mix = part(arena2, 16, 2, 2, SEQ)
        k_tok = part(arena0, 0, TT, 512)
        v_tok = part(arena0, 4, TT, 1024)
        g_tok = part(arena0, 12, TT, 2, 512)
        kc_tok = part(arena2, 0, TT, 512)
        vc_tok = part(arena2, 4, TT, 1024)
        gc_tok = part(arena2, 12, TT, 2, 512)
        z_aug = part(arena2, 20, 2 * SEQ)
        w2 = part(arena2, 22, 2, 512)
        gate_log = [part(arena0, 4, 4, 512), part(arena2, 4, 4, 512)]
        ctx_state = part(arena1, 0, HEADS, 2, DV)
        kc_tail = part(arena1, 8, TT, 2, 512)
        q_tok = part(arena1, 8, TT, 512)
        k_tail = part(arena1, 16, TT, 2, 512)
        qT = part(arena1, 24, HEADS, SEQ)
        kT = part(arena1, 28, HEADS, SEQ)
        r_tok = part(arena2, 0, TT, 1024)
        f_tok = part(arena2, 8, TT, 1024)
        qd = part(arena2, 16, 2, SEQ)
        ki = part(arena2, 18, 2, SEQ)
        states = part(arena2, 20, 2, 3, DV)
        att = part(arena2, 26, 2, TT, P)
        dec = part(arena1, 15.5, 2, 4)
        dft_cs = part(arena0, 16, 2, 512)
        o_tmp = part(arena1, 12, TT, DV)
        o_dump = part(arena1, 14, DV)
        fn_cs = part(arena2, 20, 2, 2, 512)
        h = part(arena0, 0, TT, D)
        sg = part(arena0, 16, TT, NW)
        pe_out = part(arena1, 16, TT, D)
        gate_bc = part(arena1, 8, D)
        acc = part(arena1, 16, TT, D)
        conv_v = part(arena1, 16, KC, SEQ)
        uT = part(arena2, 0, KC, SEQ + 2 * HALO)
        sq = part(arena2, 0, KC, SEQ)
        b2_row = part(arena2, 0, D)
        fin_g = part(arena2, 0, D)
        b1_row = part(arena1, 8, 2, NW)
        hid_tok = part(arena2, 18, TT, NW)
        a32_ffn = part(arena2, 22, 2, 2, SEQ)
        prod = part(arena2, 22, 4, SEQ)
        pool_acc = part(arena2, 26, SEQ)
        pool_acc2 = part(arena2, 27, SEQ)
        sq_dump = part(arena2, 20, NW)
        mean_bc = part(arena2, 26, SEQ)
        rstd_bc = part(arena2, 27, SEQ)
        diag = part(arena2, 18, NW)

        A = [stack.enter_context(nc.psum_tensor(f"A{n}", [P, 512], F32)) for n in range(4)]
        O = [stack.enter_context(nc.psum_tensor(f"O{n}", [P, 512], F32)) for n in range(2)]
        T = stack.enter_context(nc.psum_tensor("T", [P, 512], F32))
        AD = stack.enter_context(nc.psum_tensor("AD", [P, 512], F32))

        w_landed = [sem(f"w_landed{n}") for n in range(4)]
        ada_landed = [sem(f"ada_landed{n}") for n in range(2)]
        pw1_ada_landed = [sem(f"pw1_ada_landed{n}") for n in range(2)]
        start_landed = [sem(f"start_landed{n}") for n in range(5)]
        NAMES = """hi_ready lo_ready w_used ada_used rows_copied a_full tile_done a_free o_full o_free t_full t_free
            small_landed mats_landed x_landed ctx_landed cleared c_ready dve_step act_step x_ready ssq_ready
            hn_ready a32_even hi_done gain_ready w2_cleared w2_landed log_ready g_ready exp_ready sig_ready
            osq_ready gated dft_landed recip_ready y_hi root_ready h_landed diag_ready sg_ready hid_hi_ready
            h_ready b1_landed piece_done prod_ready prod_added conv_dve xc_ready sq_ready yn_ready ln_hi ln_lo
            b2_landed fin_landed result_ready stored start_used ada_summed""".split()
        (hi_ready, lo_ready, w_used, ada_used, rows_copied, a_full, tile_done, a_free, o_full, o_free, t_full,
         t_free, small_landed, mats_landed, x_landed, ctx_landed, cleared, c_ready, dve_step, act_step, x_ready,
         ssq_ready, hn_ready, a32_even, hi_done, gain_ready, w2_cleared, w2_landed, log_ready, g_ready,
         exp_ready, sig_ready, osq_ready, gated, dft_landed, recip_ready, y_hi, root_ready, h_landed, diag_ready,
         sg_ready, hid_hi_ready, h_ready, b1_landed, piece_done, prod_ready, prod_added, conv_dve, xc_ready,
         sq_ready, yn_ready, ln_hi, ln_lo, b2_landed, fin_landed, result_ready, stored, start_used, ada_summed) = [sem(name) for name in NAMES]

        ident = mats[:, M_IDENT:M_IDENT + P]
        pick = mats[:, M_PICK:M_PICK + 2]

        def mat(m):
            return mats[:, m:m + P]

        def modc(layer, what, which=0):
            o = (layer * 6 + what) * KC
            return mod[:, o:o + KC, which]

        def rows(w):
            return w.rearrange("(k p) n -> p k n", p=P)

        gm_in, gm_out = rows(gm_w_in[0]), rows(gm_w_out[0])
        pw1, pw2 = rows(cv_w_pw1[0]), rows(cv_w_pw2[0])
        f_in = [rows(ffn_w_in[n]) for n in range(2)]
        f_out = [rows(ffn_w_out[n]) for n in range(2)]
        ada = [rows(ada_w[n]) for n in range(2)]

        def tiled(v):
            return v.rearrange("(t p) n -> p t n", p=P)

        MIX = [("k", K_OFF, True), ("v", V_OFF, True), ("v", V_OFF + NW, True), ("q", Q_OFF, False),
               ("r", R_OFF, False), ("r", R_OFF + NW, False), ("f", F_OFF, False), ("f", F_OFF + NW, False)]
        START_UNITS = 8
        START_ORDER = [s + m for m in range(4) for s in (0, 4)]
        START_RING = [ada_raw[:, 0, :], ada_raw[:, 1, :]] + [w_raw[:, n, :] for n in (1, 2, 3)]
        START_SLABS = 4 * START_UNITS

        def summed_by_dve(u):
            return 8 <= u < 12 or 23 <= u < 34

        DVE_SLABS, PE_SLABS = [0], [0]
        for u in range(START_UNITS, 2 * UNITS):
            for _ in range(4):
                DVE_SLABS.append(DVE_SLABS[-1] + summed_by_dve(u))
                PE_SLABS.append(PE_SLABS[-1] + (not summed_by_dve(u)))
        MIX_UNITS_END = 23
        ADA_MIX = (0, 1, 1, 2,  1, 2, 1, 2,  2, 1, 1, 2,  1, 1, 1, 1) + 4 * (1, 2, 2, 1)
        ADA_OUT = (1, 1, 0, 1,  1, 0, 1, 1,  1, 1, 1, 1,  1, 1, 1, 1)
        FNET_ADA = 1
        ADA_FFN = (1, 0, 1, 0, 1, 0, 1, 0)
        ADA_PW1 = (0, 1, 1, 1, 1, 1, 1, 2)
        ADA_PW2 = (0, 1, 1, 1)
        TAIL_UNIT, TAIL_UNITS = 42, 3
        ADA_LOADS = ((-3,), (-2,), (-1,), (0, 1), (), (2,), (3,), (4,))
        DVE_TAPS = [31, 31, 15, 0]
        CONV_SLOTS = 8
        CONV_LIST = [(m, tap) for tap in range(CONV_W) for m in range(3) if tap < DVE_TAPS[m]]
        PROD_LIST = [(3, tap) for tap in range(CONV_W)] + [(2, tap) for tap in range(15, CONV_W)]
        PRODS = len(PROD_LIST)

        def share(total, n):
            return total * n // CONV_SLOTS, total * (n + 1) // CONV_SLOTS

        SLABS_TO_PW1 = 1 + (len(MIX) + 4) * (KC // KS) + FB * 12
        TURNS_TO_SUMS = 30
        A_MIX = (18, 22, 26, 30, 32, 35, 38, 41)
        SLABS = SLABS_TO_PW1 + 8 * 4 + 4 * 4 + FB * 12

        PW1_ADA, PW1_ADA_END = 4 * (34 - START_UNITS), 4 * (TAIL_UNIT + TAIL_UNITS - START_UNITS)

        def ada_arrival(U):
            landed, n = ada_landed, U.n
            if PW1_ADA <= n < PW1_ADA_END:
                landed, n = pw1_ada_landed, n - PW1_ADA
            elif n >= PW1_ADA_END:
                n -= PW1_ADA_END - PW1_ADA
            value = 16 * (n // 2 + 1)
            return landed[n % 2], value if U.it is None else U.it * (8 * U.per) + value

        def next_ada_slab(eng, U, src):
            n, it = U.n, U.it
            if n < 2:
                eng.wait_ge(start_used, START_SLABS - 1 + n)
            elif summed_by_dve(START_UNITS + (n - 2) // 4):
                used = 4 * DVE_SLABS[n - 1]
                eng.wait_ge(ada_summed, used if it is None else it * (4 * U.per) + used)
            else:
                used = PE_SLABS[n - 1]
                eng.wait_ge(ada_used, used if it is None else it * U.per + used)
            dst = ada_raw[:, n % 2, :].rearrange("p (k n) -> p k n", k=KS)
            eng.dma_start(dst, src).then_inc(ada_arrival(U)[0], 16)
            U.n += 1

        block = stack.enter_context(nc.Block())

        @block.sync
        def _(sp):
            S = Tally()

            def load(src):
                if S.it is not None or S.n >= 4:
                    sp.wait_ge(lo_ready, S.at(-3))
                elif S.n > 0:
                    sp.wait_ge(start_used, START_SLABS - 5 + S.n)
                dst = w_raw[:, S.n % 4, :].rearrange("p (k n) -> p k n", k=src.shape[1])
                sp.dma_start(dst, src).then_inc(w_landed[S.n % 4], 16)
                S.n += 1

            def column(w, n0, k0=0, slabs=KC // KS):
                for q in range(slabs):
                    load(w[:, k0 + KS * q:k0 + KS * (q + 1), n0:n0 + NW])

            def start_load(n):
                if n >= 5:
                    sp.wait_ge(start_used, n - 4)
                n0, q = START_ORDER[n // 4] * NW, n % 4
                sp.dma_start(START_RING[n % 5].rearrange("p (k n) -> p k n", k=KS),
                             ada[0][:, KS * q:KS * (q + 1), n0:n0 + NW]).then_inc(start_landed[n % 5], 16)

            sp.dma_start(mats[:, :], matrices).then_inc(mats_landed, 16)
            st = vec_stage
            for slot, r0, v in ((0, 0, ada_b[0]), (0, 96, c[0]), (0, 112, c_ctx), (1, 0, ada_b[1]),
                                (1, 96, norm_mix_g[0]), (1, 112, norm_mix_g[1]), (2, 0, norm_ffn_g[0]),
                                (2, 16, norm_ffn_g[1]), (2, 32, cv_b_dw[0]), (2, 48, cv_ln_g[0]),
                                (2, 64, cv_ln_b[0])):
                rws = v.shape[0] // P
                sp.dma_start(st[r0:r0 + rws, slot, :], v.rearrange("(r n) -> r n", n=P)).then_inc(small_landed, 16)
            for n in range(4):
                start_load(n)
            sp.wait_ge(cleared, 1)
            sp.dma_start(dw_stage[0:CONV_W, :], cv_w_dw[0]).then_inc(small_landed, 16)
            sp.dma_start(gla_g[:, :], gla_norm_g.broadcast_to([P, DV])).then_inc(small_landed, 16)
            sp.dma_start(x_in, tiled(x[0])).then_inc(x_landed, 16)
            sp.dma_start(pe_in, tiled(pos_embed)).then_inc(x_landed, 16)
            start_load(4)
            sp.dma_start(ctx_in, tiled(ctx[0])).then_inc(ctx_landed, 16)
            load(gm_in[:, :, Z_OFF:Z_OFF + P])
            for n in range(5, START_SLABS):
                start_load(n)
            for _, n0, _ in MIX:
                column(gm_in, n0)
            for m in range(4):
                for q in range(KC // KS):
                    load(gm_out[:, KS * q:KS * (q + 1), m * NW:(m + 1) * NW])
                    if m == 0 and q == 0:
                        sp.wait_ge(t_free, TURNS_TO_SUMS)
                        sp.dma_start(dft_cs, dft.rearrange("(t p) n -> p t n", p=P)).then_inc(dft_landed, 16)
                if m == 0:
                    sp.wait_ge(gated, HEADS * TT)
                    sp.dma_start(h, tiled(x[0])).then_inc(h_landed, 16)
                    sp.dma_start(pe_out, tiled(pos_embed)).then_inc(h_landed, 16)

            def ffn(layer):
                column(f_in[layer], 0)
                column(f_in[layer], D_FF)
                for i in loop(sp, FB - 1, (S, 12)):
                    for n0 in (0, D_FF):
                        for q in range(KC // KS):
                            load(f_in[layer][:, KS * q:KS * (q + 1), bass.ds(i * NW + (n0 + NW), NW)])
                    for m in range(4):
                        load(f_out[layer][:, bass.ds(i * KS, KS), m * NW:(m + 1) * NW])
                for m in range(4):
                    load(f_out[layer][:, KS * (FB - 1):KS * FB, m * NW:(m + 1) * NW])

            ffn(0)
            U = Tally()
            U.n = 4 * (34 - START_UNITS)

            def ada_of(cols, q):
                next_ada_slab(sp, U, ada[1][:, KS * q:KS * (q + 1), cols])

            def b1(cols):
                for half in range(2):
                    sp.dma_start(b1_row[0:1, half, :], cv_b_pw1[:, cols(half * D)]).then_inc(b1_landed, 16)

            for n in range(8):
                load(pw1[:, KS * (n % 4):KS * (n % 4 + 1), n // 4 * D:n // 4 * D + NW])
                if n == 3:
                    sp.wait_ge(h_ready, 4 * TT * 2)
                    b1(lambda o: slice(o, o + NW))
                for k in ADA_LOADS[n]:
                    if k >= 0:
                        ada_of(slice((10 + k // 4) * NW, (11 + k // 4) * NW), k % 4)
            for i in loop(sp, 3, (S, 8), (U, 8)):
                for n in range(8):
                    load(pw1[:, KS * (n % 4):KS * (n % 4 + 1), bass.ds(i * NW + (n // 4 * D + NW), NW)])
                    if n == 1:
                        sp.wait_ge(w_used, i * 8 + (SLABS_TO_PW1 + 5))
                        b1(lambda o: bass.ds(i * NW + (NW + o), NW))
                    for k in ADA_LOADS[n]:
                        ada_of(bass.ds(i * (2 * NW) + (12 + k // 4) * NW, NW), k % 4)
            for m in range(4):
                if m > 0:
                    column(pw2, m * NW)
                else:
                    for n in range(4):
                        load(pw2[:, KS * n:KS * (n + 1), 0:NW])
                        for k in ADA_LOADS[n]:
                            if k < 0:
                                ada_of(slice(17 * NW, 18 * NW), k % 4)
                    for k in range(4 * TAIL_UNITS):
                        col = (TAIL_UNIT - UNITS + k // 4) * NW
                        ada_of(slice(col, col + NW), k % 4)
                    sp.wait_ge(yn_ready, 4)
                    sp.dma_start(b2_row[0:1, :], cv_b_pw2).then_inc(b2_landed, 16)
            ffn(1)
            sp.wait_ge(h_ready, 4 * TT * 3)
            sp.dma_start(fin_g, final_norm_g.rearrange("(a n) -> a n", a=1).broadcast_to([P, D])).then_inc(fin_landed, 16)
            for t in range(TT):
                sp.wait_ge(result_ready, t + 1)
                sp.dma_start(tiled(out[0])[:, t, :], h[:, t, :]).then_inc(stored, 16)
            sp.wait_ge(stored, 16 * TT)

        @block.gpsimd
        def _(pool):
            U = Tally()
            C = Tally()

            def ada_slab(src):
                next_ada_slab(pool, U, src)

            def unit(u, first=0, last=KC // KS):
                for q in range(first, last):
                    n0 = u % UNITS * NW
                    ada_slab(ada[u // UNITS][:, KS * q:KS * (q + 1), n0:n0 + NW])

            def unit_in_loop(n0):
                for q in range(KC // KS):
                    ada_slab(ada[1][:, KS * q:KS * (q + 1), bass.ds(n0, NW)])

            pool.wait_ge(w2_cleared, 1)
            pool.dma_start(w2[0:RANK, 0, :], gate_w_f[0]).then_inc(w2_landed, 16)
            pool.dma_start(w2[RANK:2 * RANK, 1, :], gate_w_b[0]).then_inc(w2_landed, 16)
            pool.dma_start(w2[2 * RANK:2 * RANK + 1, 0, :], gate_b_f).then_inc(w2_landed, 16)
            pool.dma_start(w2[2 * RANK:2 * RANK + 1, 1, :], gate_b_b).then_inc(w2_landed, 16)
            for u in range(START_UNITS, MIX_UNITS_END):
                unit(u)
            unit(MIX_UNITS_END)
            for i in loop(pool, FB - 1, (U, 4)):
                unit_in_loop(i * NW)

            def add_products(first, last):
                for n in range(first, last):
                    start = 0 if n < CONV_W else CONV_W
                    dst = pool_acc if n < CONV_W else pool_acc2
                    if n == start:
                        continue
                    pool.wait_ge(prod_ready, C.at(2 if n == start + 1 else 1))
                    if n == start + 1:
                        nc.gpsimd.tensor_tensor(dst, prod[:, start % 4, :], prod[:, n % 4, :], ALU.add).then_inc(prod_added, 2)
                        C.n += 2
                    else:
                        pool.wait_ge(prod_added, C.at())
                        nc.gpsimd.tensor_tensor(dst, dst, prod[:, n % 4, :], ALU.add).then_inc(prod_added, 1)
                        C.n += 1

            for i in loop(pool, 3, (C, PRODS)):
                add_products(0, PRODS)
            U.n = PW1_ADA_END
            add_products(0, CONV_W)
            for u in range(TAIL_UNIT + TAIL_UNITS, 2 * UNITS):
                unit(u)

        @block.tensor
        def _(pe):
            S, A_, O_, T_ = Tally(), Tally(), Tally(), Tally()
            U = Tally()
            G, V = Tally(), Tally()
            pending = [None]
            dft_bufs = [0]

            def take_a():
                if A_.n >= 4:
                    pe.wait_ge(a_free, A_.at(-3))
                A_.n += 1
                return A[(A_.n - 1) % 4]

            def take_o():
                if O_.n >= 2:
                    pe.wait_ge(o_free, O_.at(-1))
                O_.n += 1
                return O[(O_.n - 1) % 2]

            def take_t():
                if T_.n > 0:
                    pe.wait_ge(t_free, T_.at())
                T_.n += 1
                return T

            def products(bank, hi, lo, tile, k0, first, last):
                for k in range(KS):
                    wh = w_hi[:, S.n % 2, k * NW:(k + 1) * NW]
                    wl = w_lo[:, S.n % 2, k * NW:(k + 1) * NW]
                    ah = hi[:, k0 + k, tile * P:(tile + 1) * P]
                    al = lo[:, k0 + k, tile * P:(tile + 1) * P]
                    nc.tensor.matmul(bank, ah, wh, start=first and k == 0, stop=False)
                    nc.tensor.matmul(bank, ah, wl, start=False, stop=False)
                    mm = nc.tensor.matmul(bank, al, wh, start=False, stop=last and k == KS - 1)
                return mm

            def slab(banks, sources, k0, first, last, seeded=False, take=take_a):
                pe.wait_ge(lo_ready, S.at(1))
                for n, (hi, lo, tile) in enumerate(sources):
                    if first and not seeded:
                        banks.append(take())
                    mm = products(banks[n][:, :], hi, lo, tile, k0, first and not seeded, last)
                    if last and n < len(sources) - 1:
                        mm.then_inc(tile_done, 1)
                mm.then_inc(w_used, 1)
                S.n += 1

            def ada_work(slabs=1, bank_shared=False):
                for _ in range(slabs):
                    q = U.n % 4
                    if q == 0:
                        pe.wait_ge(rows_copied, G.at())
                        if bank_shared:
                            pe.wait_ge(t_free, T_.at())
                    pe.wait_ge(*ada_arrival(U))
                    for k in range(KS):
                        mm = nc.tensor.matmul(AD[32 * k:32 * k + 32, :], c_pad[:, KS * q + k, :],
                                              ada_raw[:, U.n % 2, k * NW:(k + 1) * NW], start=q == 0,
                                              stop=q == 3, tile_position=(0, 32 * k))
                    mm.then_inc(ada_used, 1)
                    U.n += 1
                    if q == 3:
                        G.n += 1
                        pending[0] = "pe"

            def ada_skip(slabs):
                U.n += slabs
                V.n += 4 * slabs
                if slabs and U.n % 4 == 0:
                    pending[0] = "dve"

            def ada_turn():
                who, pending[0] = pending[0], None
                if who is None:
                    return
                if who == "pe":
                    pe.wait_ge(rows_copied, G.at())
                else:
                    pe.wait_ge(ada_summed, V.at())
                bank = take_t()
                for m in range(4):
                    width, right = (2, pick) if who == "pe" else (1, ones[:, 0:1])
                    mm = nc.tensor.matmul(bank[:, width * m:width * (m + 1)], ada_rows[:, m * P:(m + 1) * P], right,
                                          start=True, stop=True)
                mm.then_inc(t_full, 1)

            def norm_turn(src, wait_sem, value, pairs=range(KC // 2)):
                pe.wait_ge(wait_sem, value)
                for j in pairs:
                    bank = take_a()
                    for e in range(2):
                        for t in range(TT):
                            k = 2 * j + e
                            mm = nc.tensor.transpose(bank[:, e * SEQ + t * P:e * SEQ + (t + 1) * P],
                                                     src[:, t, k * P:(k + 1) * P], ident)
                    mm.then_inc(a_full, 1)

            def gate_quarter(m, count):
                pe.wait_ge(diag_ready, count)
                bank = take_t()
                nc.tensor.matmul(bank[:, :], ones[:, :], diag, start=True, stop=True).then_inc(t_full, 1)

            pe.wait_ge(mats_landed, 16)
            pe.wait_ge(small_landed, 16 * 13)
            bank = take_t()
            for slot, n in ((0, P), (1, P), (2, V_END - 2 * P)):
                mm = nc.tensor.transpose(bank[:, slot * P:slot * P + n], vec_stage[0:n, slot, :], ident[0:n, 0:n])
            mm.then_inc(t_full, 1)
            bank = take_t()
            for k in range(KC):
                mm = nc.tensor.transpose(bank[:, 32 * k:32 * k + 32], dw_stage[0:32, k * P:(k + 1) * P],
                                         ident[0:32, 0:32])
            mm.then_inc(t_full, 1)
            pe.wait_ge(c_ready, 1)

            def z_part(m):
                pe.wait_ge(a_free, A_.at(-4 if m < 3 else 0))
                for n, (hi, lo) in enumerate(((a_hi, a_lo), (ac_hi, ac_lo))):
                    bank = O[n]
                    for k in range(KS * m, KS * (m + 1)):
                        wh, wl = w_hi[:, 0, k * P:(k + 1) * P], w_lo[:, 0, k * P:(k + 1) * P]
                        nc.tensor.matmul(bank[:, 0:SEQ], wh, hi[:, k, :], start=k == 0, stop=False)
                        nc.tensor.matmul(bank[:, 0:SEQ], wh, lo[:, k, :], start=False, stop=False)
                        mm = nc.tensor.matmul(bank[:, 0:SEQ], wl, hi[:, k, :], start=False, stop=k == KC - 1)
                    if m == 3:
                        mm.then_inc(*((o_full, 2) if n == 0 else (w_used, 1)))

            for n in range(START_SLABS):
                q = n % 4
                if q == 0 and n > 0:
                    pe.wait_ge(rows_copied, n // 4)
                pe.wait_ge(start_landed[n % 5], 16 * (n // 5 + 1))
                for k in range(KS):
                    mm = nc.tensor.matmul(AD[32 * k:32 * k + 32, :], c_pad[:, KS * q + k, :],
                                          START_RING[n % 5][:, k * NW:(k + 1) * NW], start=q == 0,
                                          stop=q == 3, tile_position=(0, 32 * k))
                mm.then_inc(start_used, 1)
                if q == 3:
                    G.n += 1
                    pending[0] = "pe"
                    ada_turn()
                if n % 8 == 7:
                    pairs = (n // 8 * 2, n // 8 * 2 + 1)
                    norm_turn(x_in, hn_ready, 2, pairs)
                    norm_turn(ctx_in, hn_ready, 4, pairs)
                    if n > 8:
                        if n == 15:
                            pe.wait_ge(lo_ready, 1)
                        z_part(n // 8 - 1)

            lat = [(a_hi, a_lo, t) for t in range(TT)]
            both = lat + [(ac_hi, ac_lo, t) for t in range(TT)]

            z_part(3)
            A_.n += 2
            O_.n += 2
            S.n += 1

            def gate_pre(n):
                t, d = n // 2, n % 2
                bank = take_o()
                nc.tensor.matmul(bank[:, :], z_aug[0:2 * RANK + 1, t * P:(t + 1) * P], w2[0:2 * RANK + 1, d, :],
                                 start=True, stop=True).then_inc(o_full, 1)

            def ctx_tails():
                pe.wait_ge(g_ready, 2)
                for t in range(TT):
                    for d in range(2):
                        bank = take_o()
                        near = mat(M_BEFORE_ALL if d else M_AFTER_ALL)
                        far = t == d
                        mm = nc.tensor.matmul(bank[:, :], near, gc_tok[:, t, d, :], start=True, stop=not far)
                        if far:
                            mm = nc.tensor.matmul(bank[:, :], mat(M_ALL), gc_tok[:, 1 - t, d, :], start=False, stop=True)
                        mm.then_inc(o_full, 1)

            def ctx_states():
                pe.wait_ge(o_free, O_.at())
                for hd in range(HEADS):
                    bank = take_o()
                    for d in range(2):
                        for t in range(TT):
                            mm = nc.tensor.matmul(bank[:, d * DV:(d + 1) * DV], kc_tail[:, t, d, hd * DK:(hd + 1) * DK],
                                                  vc_tok[:, t, hd * DV:(hd + 1) * DV], start=t == 0, stop=t == 1)
                    mm.then_inc(o_full, 1)

            def lat_tails():
                for t in range(TT):
                    for d in range(2):
                        bank = take_o()
                        nc.tensor.matmul(bank[:, :], mat(M_BEFORE if d else M_AFTER), g_tok[:, t, d, :],
                                         start=True, stop=True).then_inc(o_full, 1)

            def turn_qk():
                for src in (q_tok, k_tok):
                    for t in range(TT):
                        bank = take_t()
                        for hd in range(HEADS):
                            mm = nc.tensor.transpose(bank[:, hd * P:(hd + 1) * P], src[:, t, hd * DK:(hd + 1) * DK], ident)
                        mm.then_inc(t_full, 1)

            def head_sums(hd):
                bank = take_t()
                for d in range(2):
                    for t in range(TT):
                        mm = nc.tensor.matmul(bank[:, d * SEQ + t * P:d * SEQ + (t + 1) * P],
                                              g_tok[:, t, d, hd * DK:(hd + 1) * DK], mat(M_INC_B if d else M_INC_F),
                                              start=True, stop=True)
                mm.then_inc(t_full, 1)

            def head_scores(hd):
                bank = take_t()
                for d in range(2):
                    for t in range(TT):
                        n = (d * TT + t) * P
                        mm = nc.tensor.matmul(bank[:, n:n + P], ki[:, d, t * P:(t + 1) * P], qd[:, d, t * P:(t + 1) * P],
                                              start=True, stop=True)
                mm.then_inc(t_full, 1)

            def head_update(hd, m):
                for d in range(2):
                    bank = take_o()
                    ch = 3 - m if d else m
                    t, r = ch // 2, CHUNK * (ch % 2)
                    mm = nc.tensor.matmul(bank[:, 0:DV], k_tail[r:r + CHUNK, t, d, hd * DK:(hd + 1) * DK],
                                          v_tok[r:r + CHUNK, t, hd * DV:(hd + 1) * DV], start=True, stop=True)
                    mm.then_inc(o_full, 1)

            def head_out(hd):
                pe.wait_ge(t_free, T_.at())
                pe.wait_ge(o_free, O_.at())
                bank = take_a()
                for t in range(TT):
                    ps = bank[:, t * DV:(t + 1) * DV]
                    for d in range(2):
                        nc.tensor.matmul(ps, att[:, d, t, :], v_tok[:, t, hd * DV:(hd + 1) * DV],
                                         start=t == 0 and d == 0, stop=False, skip_group_check=True)
                    for half in range(2):
                        ch = 2 * t + half
                        for d in range(2):
                            n = 3 - ch if d else ch
                            state = ctx_state[:, hd, d, :] if n == 0 else states[:, d, n - 1, :]
                            mm = nc.tensor.matmul(ps[half * CHUNK:(half + 1) * CHUNK, :],
                                                  qd[:, d, ch * CHUNK:(ch + 1) * CHUNK], state,
                                                  start=False, stop=d == 1, skip_group_check=True)
                mm.then_inc(a_full, 1)

            for n, (what, _, shared) in enumerate(MIX):
                banks = []
                for q in range(KC // KS):
                    slab(banks, both if shared else lat, KS * q, q == 0, q == 3)
                    ada_turn()
                    if n == 0:
                        if q == 0:
                            pe.wait_ge(a_free, A_.at(-4))
                            pe.wait_ge(w2_landed, 64)
                        gate_pre(2 * q)
                        gate_pre(2 * q + 1)
                    if n == 3:
                        (ctx_tails, ctx_states, lat_tails, lambda: None)[q]()
                    if n == 4 and q == 0:
                        pe.wait_ge(a_free, A_.at(-2))
                        turn_qk()
                    if n >= 4:
                        hd = n - 4
                        if q == 0:
                            head_sums(hd)
                        if q == 1:
                            head_scores(hd)
                            head_update(hd, 0)
                        if q == 2:
                            head_update(hd, 1)
                            head_update(hd, 2)
                        if q == 3:
                            head_out(hd)
                    if n == 7 and q == 0:
                        assert T_.n == TURNS_TO_SUMS
                    (ada_skip if shared else ada_work)(ADA_MIX[4 * n + q])

            def fnet(g):
                for dc in range(2):
                    bank = take_o()
                    for t in range(TT):
                        col = g * FN_W + dc * P
                        mm = nc.tensor.matmul(bank[:, :], f_tok[:, t, col:col + P], dft_cs[:, t, :], start=t == 0, stop=t == 1)
                    mm.then_inc(o_full, 1)
                pe.wait_ge(o_free, O_.at())
                bank = take_t()
                for e in range(2):
                    for dc in range(2):
                        nc.tensor.matmul(bank[:, e * SEQ:(e + 1) * SEQ], dft_cs[:, dc, e * P:(e + 1) * P],
                                         fn_cs[:, g % 2, dc, 0:SEQ], start=dc == 0, stop=False)
                        mm = nc.tensor.matmul(bank[:, e * SEQ:(e + 1) * SEQ], dft_cs[:, dc, FN_W + e * P:FN_W + (e + 1) * P],
                                              fn_cs[:, g % 2, dc, SEQ:2 * SEQ], start=False, stop=dc == 1)
                mm.then_inc(t_full, 1)

            pe.wait_ge(dft_landed, 16)
            pe.wait_ge(a_free, A_.at(-1))
            fnet(0)
            fnet(1)
            pe.wait_ge(gated, HEADS * TT)
            for j in range(4):
                bank = take_t()
                for e in range(2):
                    for t in range(TT):
                        k = 2 * j + e
                        mm = nc.tensor.transpose(bank[:, e * SEQ + t * P:e * SEQ + (t + 1) * P],
                                                 r_tok[:, t, k * P:(k + 1) * P], ident)
                mm.then_inc(t_full, 1)

            pe.wait_ge(t_free, T_.at())
            for m in range(4):
                banks = []
                for q in range(KC // KS):
                    if m == 0 and q == 2:
                        pe.wait_ge(t_free, T_.at())
                    slab(banks, lat, KS * q, q == 0, q == 3)
                    ada_turn()
                    if q == 0:
                        gate_quarter(m, m + 1)
                    ada_work(ADA_OUT[4 * m + q])
                    if m == 0 and q < 2:
                        fnet(2 + q)
                        ada_work(FNET_ADA)
            ada_turn()
            assert U.n == 4 * (MIX_UNITS_END - START_UNITS)

            hid = [(hid_hi, hid_lo, t) for t in range(TT)]

            def turn_hidden():
                pe.wait_ge(a_free, A_.at())
                for t in range(TT):
                    bank = T if t == 0 else AD
                    if t == 0:
                        take_t()
                    else:
                        T_.n += 1
                    for m in range(KS):
                        mm = nc.tensor.transpose(bank[:, m * P:(m + 1) * P], hid_tok[:, t, m * P:(m + 1) * P], ident)
                    mm.then_inc(t_full, 1)

            def ffn(layer, diags):
                norm_turn(acc, hn_ready, 6 if layer == 0 else 10)
                first = A_.n

                def block_in(head):
                    for half in range(2):
                        banks = []
                        for q in range(KC // KS):
                            if head and half == 0:
                                pe.wait_ge(a_free, first - 6 + 2 * q)
                            slab(banks, lat, KS * q, q == 0, q == 3)
                            if layer == 0:
                                ada_turn()
                                ada_skip(ADA_FFN[4 * half + q])

                block_in(True)
                turn_hidden()
                steps = [(S, 12), (A_, 4), (O_, 8)] + ([(T_, 3), (U, 4), (V, 16)] if layer == 0 else [(T_, 2)])
                for i in loop(pe, FB - 1, *steps):
                    block_in(False)
                    pe.wait_ge(t_free, T_.at(-1 if layer == 0 else 0))
                    for m in range(4):
                        slab([], hid, 0, True, True, take=take_o)
                    turn_hidden()
                pe.wait_ge(t_free, T_.at())
                for m in range(4):
                    slab([], hid, 0, True, True, take=take_o)
                    gate_quarter(m, diags + m + 1)

            ffn(0, 4)

            norm_turn(acc, hn_ready, 8)
            first = A_.n
            B = Tally()

            def turn_glu(t):
                bank = AD if t else take_t()
                T_.n += t
                for m in range(KS):
                    mm = nc.tensor.transpose(bank[:, m * P:(m + 1) * P], hid_tok[:, t, m * P:(m + 1) * P], ident)
                mm.then_inc(t_full, 1)

            def pw1_block(head):
                for half in range(2):
                    banks = []
                    for q in range(KC // KS):
                        if q == 0:
                            if half == 0:
                                pe.wait_ge(b1_landed, B.at(32))
                            for t in range(TT):
                                banks.append(take_a())
                                nc.tensor.matmul(banks[t][:, :], ones[0:1, :], b1_row[0:1, half, :], start=True, stop=False)
                        if head and half == 0:
                            pe.wait_ge(a_free, first - 6 + 2 * q)
                        slab(banks, lat, KS * q, q == 0, q == 3, seeded=True)
                        n = half * 4 + q
                        ada_turn()
                        if not head and n == 0:
                            pe.wait_ge(a_free, A_.at(-2))
                            turn_glu(0)
                            pe.wait_ge(rows_copied, G.at())
                            turn_glu(1)
                        ada_work(ADA_PW1[n], bank_shared=True)
                B.n += 32

            pw1_block(True)
            for i in loop(pe, 3, (S, 8), (A_, 4), (T_, 4), (U, 8), (G, 2), (B, 32)):
                pw1_block(False)
            ada_turn()
            pe.wait_ge(a_free, A_.at())
            turn_glu(0)
            pe.wait_ge(rows_copied, G.at())
            turn_glu(1)
            for _ in range(TAIL_UNITS - 1):
                ada_work(4, bank_shared=True)
                ada_turn()
            bank = take_o()
            for k in range(KC):
                if k % KS == 0:
                    pe.wait_ge(conv_dve, (len(CONV_LIST) + 1) * (k // KS) + (len(CONV_LIST) + 1 if k < KC - KS else CONV_W * (KS - 1)))
                    pe.wait_ge(piece_done, k // KS + 1)
                mm = nc.tensor.matmul(bank[:, 0:SEQ], ones[:, :], conv_v[:, k, :], start=k == 0, stop=k == KC - 1)
            mm.then_inc(o_full, 1)
            ada_work(2)
            bank = take_o()
            for k in range(KC):
                if k % KS == 0:
                    pe.wait_ge(sq_ready, k // KS + 1)
                mm = nc.tensor.matmul(bank[:, 0:SEQ], ones[:, :], sq[:, k, :], start=k == 0, stop=k == KC - 1)
            mm.then_inc(o_full, 1)
            ada_work(2)
            for m in range(4):
                banks = []
                for q in range(KC // KS):
                    if m == 0:
                        pe.wait_ge(ln_lo, 2 * q + 2)
                    if q == 0:
                        if m == 0:
                            pe.wait_ge(b2_landed, 16)
                        for t in range(TT):
                            banks.append(take_a())
                            nc.tensor.matmul(banks[t][:, :], ones[0:1, :], b2_row[0:1, m * NW:(m + 1) * NW], start=True, stop=False)
                    slab(banks, lat, KS * q, q == 0, q == 3, seeded=True)
                    ada_turn()
                    if q == 0:
                        gate_quarter(m, 8 + m + 1)
                    ada_work(ADA_PW2[q])
            ada_turn()
            assert U.n == 4 * (2 * UNITS - START_UNITS)
            ffn(1, 12)

        @block.scalar
        def _(act):
            S, W, D_, F, T_, O_ = Tally(), Tally(), Tally(), Tally(), Tally(), Tally()
            step = [0]
            W.n = -1

            def split():
                W.n += 1
                if S.n == SLABS:
                    return
                act.wait_ge(w_landed[S.n % 4], S.landed(4))
                if S.it is not None or S.n >= 2:
                    act.wait_ge(w_used, S.at(-1))
                nc.scalar.activation(w_hi[:, S.n % 2, :], w_raw[:, S.n % 4, :], ACT.Copy).then_inc(hi_ready, 1)
                S.n += 1

            def tile_ends(last):
                if last:
                    act.wait_ge(w_used, W.at())
                else:
                    act.wait_ge(tile_done, D_.at(1))
                    D_.n += 1

            def chained(ins):
                step[0] += 1
                ins.then_inc(act_step, 1)
                act.wait_ge(act_step, step[0])

            def root(v):
                R.n += 1
                act.wait_ge(recip_ready, R.n)
                nc.scalar.activation(v, v, ACT.Sqrt).then_inc(root_ready, 1)

            R = Tally()

            def sums_of_squares(src, dump, sem_, values, slot):
                for t in range(TT):
                    act.wait_ge(sem_, values[t])
                    nc.scalar.activation(dump[:, t, :], src[:, t, :], ACT.Square,
                                         accum_out=ssq[:, slot + t:slot + t + 1]).then_inc(ssq_ready, 1)
                root(rstd[:, slot:slot + TT])

            SQ = Tally()

            def quarter_squares(m, phase):
                for t in range(TT):
                    act.wait_ge(h_ready, 4 * TT * phase + TT * m + t + 1)
                    act.wait_ge(ssq_ready, 2 * TT + SQ.n)
                    nc.scalar.activation(sq_dump, h[:, t, m * NW:(m + 1) * NW], ACT.Square,
                                         accum_out=ssq[:, 8 + TT * m + t:9 + TT * m + t]).then_inc(ssq_ready, 1)
                    SQ.n += 1

            N = Tally()
            FREE = Tally()

            def norm_out(hi, add, a32, g=gain, pairs=range(KC // 2)):
                for j in pairs:
                    k = 2 * j + 1
                    act.wait_ge(a_full, F.at(1))
                    F.n += 1
                    if FREE.n >= 2:
                        act.wait_ge(a_free, FREE.n - 1)
                    N.n += 1
                    act.wait_ge(a32_even, N.n)
                    chained(nc.scalar.activation(a32[:, j % 2, 1, :], A[FREE.n % 4][:, SEQ:2 * SEQ], ACT.Identity,
                                                 bias=add[:, k:k + 1], scale=g[:, k:k + 1]))
                    nc.scalar.activation(hi[:, 2 * j:2 * j + 2, :], a32[:, j % 2, :, :], ACT.Copy).then_inc(hi_done, 1)
                    FREE.n += 1

            act.wait_ge(cleared, 3)
            nc.scalar.activation(c_pad[:, :, 0:2], vecs[:, V_C:V_C + 2 * KC].rearrange("p (w k) -> p k w", w=2),
                                 ACT.Silu).then_inc(c_ready, 1)
            sums_of_squares(x_in, pe_in, x_ready, (1, 2), 0)
            act.wait_ge(ctx_landed, 16)
            sums_of_squares(ctx_in, pe_in, x_ready, (2, 2), 2)
            split()
            for m in range(4):
                pairs = (2 * m, 2 * m + 1)
                act.wait_ge(gain_ready, 2 * (m + 1))
                norm_out(a_hi, modc(0, SHIFT_MIX), a32_mix, gain, pairs)
                norm_out(ac_hi, modc(0, SHIFT_MIX, 1), a32_mix, gain_ctx, pairs)
            split()
            O_.n += 2

            def gate_abs(n):
                act.wait_ge(o_full, O_.at(1))
                nc.scalar.activation(gate_log[n // 4][:, n % 4, :], O[O_.n % 2][:, :], ACT.Abs).then_inc(log_ready, 1)
                O_.n += 1

            def tails(dst):
                for t in range(TT):
                    for d in range(2):
                        act.wait_ge(o_full, O_.at(1))
                        nc.scalar.activation(dst[:, t, d, :], O[O_.n % 2][:, :], ACT.Exp).then_inc(exp_ready, 1)
                        O_.n += 1

            def head_exps(hd):
                act.wait_ge(t_full, T_.at(1))
                T_.n += 1
                both_d = T[:, :].rearrange("p (d s) -> p d s", d=2)
                nc.scalar.activation(qd, both_d, ACT.Exp)
                nc.scalar.activation(ki, both_d, ACT.Exp, scale=-1.0).then_inc(exp_ready, 1)

            def y_out(k0):
                act.wait_ge(t_full, T_.at(1))
                nc.scalar.activation(a_hi[:, k0:k0 + 2, :], T[:, :].rearrange("p (k s) -> p k s", k=2),
                                     ACT.Copy).then_inc(y_hi, 1)
                T_.n += 1

            ad = Ada()
            T_.n = 2 + START_UNITS
            ad.slabs = 4 * START_UNITS
            for n, (what, n0, shared) in enumerate(MIX):
                for q in range(KC // KS):
                    split()
                    T_.n += ad.turned()
                    if n == 0:
                        gate_abs(2 * q)
                        gate_abs(2 * q + 1)
                    if n == 1 and q == 0:
                        act.wait_ge(log_ready, 8)
                        for g in gate_log:
                            chained(nc.scalar.activation(g, g, ACT.Exp, scale=-1.0))
                    if n == 1 and q == 1:
                        for g in gate_log:
                            nc.scalar.activation(g, g, ACT.Ln, bias=1.0).then_inc(log_ready, 1)
                    if q == 3:
                        tiles = 2 * TT if shared else TT
                        for t in range(tiles):
                            if what == "r":
                                tile_ends(t == tiles - 1)
                                nc.scalar.activation(r_tok[:, t, n0 - R_OFF:n0 - R_OFF + NW], A[(A_MIX[n] + t) % 4][:, :],
                                                     ACT.Sigmoid).then_inc(sig_ready, 1)
                            elif t < tiles - 1:
                                D_.n += 1
                    if n == 3 and q == 0:
                        tails(kc_tail)
                    if n == 3 and q == 1:
                        O_.n += HEADS
                    if n == 3 and q == 2:
                        tails(k_tail)
                    if n == 4 and q == 0:
                        T_.n += 4
                    if n >= 4:
                        if q == 0:
                            head_exps(n - 4)
                        if q == 1:
                            T_.n += 1
                            O_.n += 2
                        if q == 2:
                            O_.n += 4
                        if q == 3:
                            act.wait_ge(a_full, F.at(1))
                            F.n += 1
                            if n > 4:
                                act.wait_ge(a_free, A_MIX[n - 1] + 3)
                            for t in range(TT):
                                if t == 1:
                                    act.wait_ge(osq_ready, TT * (n - 4) + 1)
                                nc.scalar.activation(o_dump, A[(A_MIX[n] + 2) % 4][:, t * DV:(t + 1) * DV], ACT.Square,
                                                     accum_out=ssq[:, 4 + t:5 + t]).then_inc(osq_ready, 1)
                            root(rstd[:, 4:4 + TT])
                    ad.work(ADA_MIX[4 * n + q])

            for g in range(2):
                O_.n += 2
                y_out(8 + 2 * g)
            for j in range(4):
                y_out(2 * j)
            for m in range(4):
                for q in range(KC // KS):
                    split()
                    T_.n += ad.turned() + (q == 0)
                    if m > 0 and q == 0:
                        quarter_squares(m - 1, 0)
                    ad.work(ADA_OUT[4 * m + q])
                    if m == 0 and q < 2:
                        O_.n += 2
                        y_out(12 + 2 * q)
                        ad.work(FNET_ADA)
                D_.n += 1
            T_.n += ad.turned()

            def ffn(layer):
                quarter_squares(3, 2 * layer)
                root(rstd[:, 0:TT])
                act.wait_ge(gain_ready, 9 + 2 * layer)
                norm_out(a_hi, modc(layer, SHIFT_FFN), a32_ffn)

                def block_in():
                    for n in range(8):
                        split()
                        if layer == 0:
                            T_.n += ad.turned()
                            ad.work(ADA_FFN[n])
                        if n == 3:
                            for t in range(TT):
                                tile_ends(t == TT - 1)
                                nc.scalar.activation(sg[:, t, :], A[t][:, :], ACT.Silu).then_inc(sg_ready, 1)
                    D_.n += 1

                def hidden_hi():
                    for t, bank in enumerate((T, AD)):
                        act.wait_ge(t_full, T_.at(1))
                        nc.scalar.activation(hid_hi[:, :, t * P:(t + 1) * P],
                                             bank[:, :].rearrange("p (k s) -> p k s", k=KS), ACT.Copy).then_inc(hid_hi_ready, 1)
                        T_.n += 1

                block_in()
                hidden_hi()
                for i in loop(act, FB - 1, (S, 12), (W, 12), (D_, 6), (T_, 3 if layer == 0 else 2)):
                    block_in()
                    for m in range(4):
                        split()
                        D_.n += 1
                    hidden_hi()
                for m in range(4):
                    split()
                    D_.n += 1
                    T_.n += 1
                    if m > 0:
                        quarter_squares(m - 1, 2 * layer + 1)

            FREE.n = A_MIX[-1] + 3 + 8
            ffn(0)

            quarter_squares(3, 1)
            root(rstd[:, 0:TT])
            act.wait_ge(gain_ready, 10)
            FREE.n += 4 * FB
            norm_out(a_hi, modc(1, SHIFT_MIX), a32_ffn)
            C = Tally()

            def conv_products(piece, b_col, first, last):
                for n in range(first, last):
                    m, tap = PROD_LIST[n]
                    if n == 0:
                        act.wait_ge(t_free, T_.at())
                    if C.n > 0 or C.it is not None:
                        if n == 0 or n >= 4:
                            act.wait_ge(prod_added, C.at(0 if n == 0 else -3))
                    w = w_dw[:, piece(m), tap:tap + 1].rearrange("p a b -> p (a b)")
                    dst = prod[:, n % 4:n % 4 + 1, :]
                    src = uT[:, piece(m), tap:tap + SEQ]
                    if n == 0:
                        nc.scalar.activation(dst, src, ACT.Identity, scale=w, bias=b_col).then_inc(prod_ready, 1)
                    else:
                        nc.scalar.activation(dst, src, ACT.Copy, scale=w).then_inc(prod_ready, 1)
                    C.n += 1
                    if n == CONV_W - 1:
                        act.wait_ge(prod_added, C.at())
                        nc.scalar.activation(conv_v[:, piece(3), :], pool_acc[:, None, :], ACT.Copy).then_inc(piece_done, 1)

            def pw1_block(piece, b_col):
                for n in range(8):
                    split()
                    T_.n += ad.turned()
                    if piece is not None:
                        T_.n += 2 * (n == 0)
                        conv_products(piece, b_col, *share(PRODS, n))
                    if n == 3:
                        D_.n += 1
                    if n == 7:
                        for t in range(TT):
                            tile_ends(t == TT - 1)
                            nc.scalar.activation(sg[:, t, :], A[2 + t][:, :], ACT.Sigmoid).then_inc(sg_ready, 1)
                    ad.work(ADA_PW1[n])

            ad.slabs = 4 * 34
            pw1_block(None, None)
            for i in loop(act, 3, (S, 8), (W, 8), (D_, 2), (T_, 4), (C, PRODS)):
                pw1_block(lambda m: bass.ds(i * KS + m, 1), vecs[:, bass.ds(i * KS + (V_BDW + KS - 1), 1)])
            T_.n += ad.turned() + 2
            conv_products(lambda m: slice(KC - KS + m, KC - KS + m + 1), vecs[:, V_LNG - 1:V_LNG], 0, CONV_W)
            for _ in range(TAIL_UNITS - 1):
                ad.work(4)
                T_.n += ad.turned()
            ad.work(4)
            for g in range(4):
                act.wait_ge(xc_ready, g + 1)
                nc.scalar.activation(sq[:, 4 * g:4 * g + 4, :], conv_v[:, 4 * g:4 * g + 4, :], ACT.Square).then_inc(sq_ready, 1)
            root(rstd_bc)
            for j in range(KC // 2):
                act.wait_ge(yn_ready, j // 2 + 1)
                if j >= 2:
                    act.wait_ge(ln_lo, j - 1)
                for e in range(2):
                    k = 2 * j + e
                    chained(nc.scalar.activation(a32_ffn[:, j % 2, e, :], conv_v[:, k, :], ACT.Silu,
                                                 bias=vecs[:, V_LNB + k:V_LNB + k + 1], scale=vecs[:, V_LNG + k:V_LNG + k + 1]))
                nc.scalar.activation(a_hi[:, 2 * j:2 * j + 2, :], a32_ffn[:, j % 2, :, :], ACT.Copy).then_inc(ln_hi, 1)
            for m in range(4):
                for q in range(KC // KS):
                    split()
                    T_.n += ad.turned() + (q == 0)
                    if m > 0 and q == 0:
                        quarter_squares(m - 1, 2)
                    ad.work(ADA_PW2[q])
                D_.n += 1
            T_.n += ad.turned()
            FREE.n = FREE.n + 16 + 8
            ffn(1)
            quarter_squares(3, 3)
            root(rstd[:, 0:TT])

        @block.vector
        def _(dve):
            S, W, D_, F, T_, O_, FREE, OW = Tally(), Tally(), Tally(), Tally(), Tally(), Tally(), Tally(), Tally()
            G, SIG, SG, H, X = Tally(), Tally(), Tally(), Tally(), Tally()
            step, norms, ssqs = [0], [0], [0]
            W.n = -1

            def split():
                W.n += 1
                if S.n == SLABS:
                    return
                dve.wait_ge(hi_ready, S.at(1))
                nc.vector.tensor_tensor(w_lo[:, S.n % 2, :], w_raw[:, S.n % 4, :], w_hi[:, S.n % 2, :].bitcast(F32),
                                        ALU.subtract).then_inc(lo_ready, 1)
                S.n += 1

            def tile_ends(last):
                if last:
                    dve.wait_ge(w_used, W.at())
                else:
                    dve.wait_ge(tile_done, D_.at(1))
                    D_.n += 1

            def chained(ins):
                step[0] += 1
                ins.then_inc(dve_step, 1)
                dve.wait_ge(dve_step, step[0])

            def t_whole():
                dve.wait_ge(t_full, T_.at(1))
                T_.n += 1

            def o_whole():
                OW.n += 1
                dve.wait_ge(o_full, OW.at())
                O_.n += 1
                return O[(O_.n - 1) % 2]

            def freed():
                FREE.n += 1
                return A[(FREE.n - 1) % 4]

            ad = Ada()

            def ada_add(offset=None):
                t_whole()
                dst = mod[:, (G.n - 1) * 4:G.n * 4, :] if offset is None else mod[:, bass.ds(offset, 4), :]
                if G.it is None and not summed_by_dve(G.n - 1) or G.it is not None and not summed_by_dve(G.n):
                    turned = T[:, 0:8].rearrange("p (k w) -> p k w", w=2)
                else:
                    dst, turned = dst[:, :, 0:1], T[:, 0:4].rearrange("p (k w) -> p k w", w=1)
                nc.vector.tensor_tensor(dst, dst, turned, ALU.add).then_inc(t_free, 1)

            def ada_copy(sem_=ada_used, value=None):
                G.n += 1
                if value is None:
                    value = USED.at(4)
                    USED.n += 4
                    U.n += 4
                dve.wait_ge(sem_, value)
                nc.vector.tensor_copy(ada_rows[:, :], AD[:, :]).then_inc(rows_copied, 1)

            USED = Tally()
            U, V = Tally(), Tally()

            def ada_sum(slabs):
                for _ in range(slabs):
                    q = U.n % 4
                    dve.wait_ge(*ada_arrival(U))
                    for k in range(KS):
                        w, cc = ada_raw[:, U.n % 2, k * NW:(k + 1) * NW], c_pad[:, KS * q + k, 0:1]
                        if q == 0 and k == 0:
                            nc.vector.tensor_scalar(ada_rows[:, :], w, cc, None, ALU.mult).then_inc(ada_summed, 1)
                        else:
                            dve.wait_ge(ada_summed, V.at())
                            nc.vector.scalar_tensor_tensor(out=ada_rows[:, :], in0=w, scalar=cc, in1=ada_rows[:, :],
                                                           op0=ALU.mult, op1=ALU.add).then_inc(ada_summed, 1)
                        V.n += 1
                    U.n += 1
                    if q == 3:
                        G.n += 1

            def inverse_root(v):
                nc.vector.reciprocal(v, v).then_inc(recip_ready, 1)
                R.n += 1
                dve.wait_ge(root_ready, R.n)

            R = Tally()

            def inverse_rms(slot, n, width):
                chained(nc.vector.tensor_scalar(rstd[:, slot:slot + n], ssq[:, slot:slot + n], 1.0 / width, EPS, ALU.mult, ALU.add))
                inverse_root(rstd[:, slot:slot + n])

            def h_squares():
                ssqs[0] += 4 * TT
                dve.wait_ge(ssq_ready, ssqs[0])
                chained(nc.vector.tensor_tensor(ssq[:, 8:12], ssq[:, 8:12], ssq[:, 12:16], ALU.add))
                chained(nc.vector.tensor_tensor(ssq[:, 0:2], ssq[:, 8:10], ssq[:, 10:12], ALU.add))

            def normed(dst, src, slot):
                if src is h:
                    h_squares()
                else:
                    ssqs[0] += TT
                    dve.wait_ge(ssq_ready, ssqs[0])
                inverse_rms(slot, TT, D)
                for t in range(TT):
                    nc.vector.tensor_scalar(dst[:, t, :], src[:, t, :], rstd[:, slot + t:slot + t + 1], None,
                                            ALU.mult).then_inc(hn_ready, 1)

            def set_gain(layer, what, g0, which=0, k0=0, k1=KC):
                dst = gain_ctx if which else gain
                nc.vector.scalar_tensor_tensor(out=dst[:, k0:k1], in0=modc(layer, what, which)[:, k0:k1], scalar=1.0,
                                               in1=vecs[:, g0 + k0:g0 + k1], op0=ALU.add, op1=ALU.mult).then_inc(gain_ready, 1)
                norms[0] += 1
                dve.wait_ge(gain_ready, norms[0])

            def norm_out(hi, lo, add, a32, g=gain, pairs=range(KC // 2)):
                def lo_part(j):
                    X.n += 1
                    dve.wait_ge(hi_done, X.n)
                    nc.vector.tensor_tensor(lo[:, 2 * j:2 * j + 2, :], a32[:, j % 2, :, :], hi[:, 2 * j:2 * j + 2, :].bitcast(F32),
                                            ALU.subtract).then_inc(a_free, 1)

                for j in pairs:
                    k = 2 * j
                    dve.wait_ge(a_full, F.at(1))
                    F.n += 1
                    if FREE.n >= 2:
                        dve.wait_ge(a_free, FREE.n - 1)
                    nc.vector.tensor_scalar(a32[:, j % 2, 0, :], freed()[:, 0:SEQ], g[:, k:k + 1], add[:, k:k + 1],
                                            ALU.mult, ALU.add).then_inc(a32_even, 1)
                    if j > pairs[0]:
                        lo_part(j - 1)
                lo_part(pairs[-1])

            def diagonal(layer, what, m, last=False):
                for k in range(KS):
                    ins = nc.vector.tensor_scalar(diag[:, k * P:(k + 1) * P], ident, modc(layer, what)[:, m * KS + k:m * KS + k + 1],
                                                  None, ALU.mult)
                ins.then_inc(diag_ready, 1)

            def gate_quarter(layer, what, m):
                t_whole()
                nc.vector.tensor_copy(gate_bc[:, m * NW:(m + 1) * NW], T[:, :]).then_inc(t_free, 1)
                if m < 3:
                    diagonal(layer, what, m + 1)

            def residual(t, m):
                cols = slice(m * NW, (m + 1) * NW)
                tile_ends(t == TT - 1)
                nc.vector.tensor_tensor(sg[:, t, :], freed()[:, :], gate_bc[:, cols], ALU.mult).then_inc(a_free, 1)
                dve.wait_ge(a_free, FREE.at())
                nc.vector.tensor_tensor(h[:, t, cols], h[:, t, cols], sg[:, t, :], ALU.add).then_inc(h_ready, 1)

            nc.vector.memset(dw_stage[0:32, :], 0.0).then_inc(cleared, 1)
            nc.vector.memset(w2[0:2 * RANK + 1, :, :], 0.0).then_inc(w2_cleared, 1)
            nc.vector.memset(ones[:, :], 1.0)
            nc.vector.memset(z_aug[0:2 * RANK + 1, :], 1.0)
            nc.vector.memset(c_pad[:, :, :], 0.0).then_inc(cleared, 1)
            t_whole()
            nc.vector.tensor_copy(vecs[:, :], T[:, 0:V_END]).then_inc(t_free, 1)
            dve.wait_ge(t_free, 1)
            for w in range(2):
                for layer, v0 in ((0, V_ADAB0), (1, V_ADAB1)):
                    ins = nc.vector.tensor_copy(mod[:, layer * 6 * KC:(layer + 1) * 6 * KC, w], vecs[:, v0:v0 + 6 * KC])
            ins.then_inc(cleared, 1)
            t_whole()
            nc.vector.tensor_copy(w_dw[:, :, :], T[:, :].rearrange("p (k t) -> p k t", k=KC)).then_inc(t_free, 1)
            dve.wait_ge(x_landed, 32)
            for t in range(TT):
                nc.vector.tensor_tensor(x_in[:, t, :], x_in[:, t, :], pe_in[:, t, :], ALU.add).then_inc(x_ready, 1)
            normed(x_in, x_in, 0)
            normed(ctx_in, ctx_in, 2)
            for n, u in enumerate(START_ORDER):
                ada_copy(start_used, 4 * (n + 1))
                ada_add(4 * u)
                if n == 0:
                    split()
                if n % 2 == 1:
                    dve.wait_ge(t_free, T_.at())
                    k0, pairs = (n // 2) * KS, (n - 1, n)
                    set_gain(0, SCALE_MIX, V_MIXG, 0, k0, k0 + KS)
                    set_gain(0, SCALE_MIX, V_MIXG, 1, k0, k0 + KS)
                    norm_out(a_hi, a_lo, modc(0, SHIFT_MIX), a32_mix, gain, pairs)
                    norm_out(ac_hi, ac_lo, modc(0, SHIFT_MIX, 1), a32_mix, gain_ctx, pairs)
            split()
            dve.wait_ge(c_ready, 1)
            for n in range(2):
                dve.wait_ge(*((o_full, 2) if n == 0 else (w_used, 1)))
                nc.vector.tensor_copy(z_aug[0:2 * RANK, n * SEQ:(n + 1) * SEQ],
                                      O[n][0:2 * RANK, 0:SEQ]).then_inc(a_free if n else o_free, 2)
            FREE.n += 2
            O_.n += 2
            OW.n += 2

            E = Tally()

            def log_gate(n):
                t, d = n // 2, n % 2
                dst = (g_tok[:, t, d, :] if t < TT else gc_tok[:, t - TT, d, :])
                bank = o_whole()
                dve.wait_ge(log_ready, n + 1)
                nc.vector.tensor_scalar(dst, bank[:, :], 0.0, None, ALU.min).then_inc(o_free, 1)

            def finish_log_gates():
                dve.wait_ge(log_ready, 10)
                dve.wait_ge(o_free, 2 + 8)
                for n, g in enumerate((g_tok, gc_tok)):
                    flat = g.rearrange("p t d k -> p (t d) k")
                    nc.vector.tensor_tensor(flat, flat, gate_log[n], ALU.subtract).then_inc(g_ready, 1)

            def tails(dst, keys):
                for t in range(TT):
                    for d in range(2):
                        o_whole()
                        E.n += 1
                        dve.wait_ge(exp_ready, E.n)
                        nc.vector.tensor_tensor(dst[:, t, d, :], dst[:, t, d, :], keys[:, t, :], ALU.mult).then_inc(o_free, 1)

            def head_decays(hd):
                t_whole()
                E.n += 1
                dve.wait_ge(exp_ready, E.n)
                nc.vector.tensor_copy(dec[:, 0, :], qd[:, 0, :].rearrange("p (c s) -> p c s", s=CHUNK)[:, :, CHUNK - 1])
                chained(nc.vector.tensor_copy(dec[:, 1, :], qd[:, 1, :].rearrange("p (c s) -> p c s", s=CHUNK)[:, :, 0]))
                for d in range(2):
                    nc.vector.tensor_tensor(ki[:, d, :], ki[:, d, :], kT[:, hd, :], ALU.mult)
                    ins = nc.vector.tensor_tensor(qd[:, d, :], qd[:, d, :], qT[:, hd, :], ALU.mult)
                ins.then_inc(t_free, 1)

            def head_mask(hd):
                t_whole()
                for d in range(2):
                    for t in range(TT):
                        n = (d * TT + t) * P
                        ins = nc.vector.copy_predicated(att[:, d, t, :], mat(M_INC_B if d else M_INC_F).bitcast(U32),
                                                        T[:, n:n + P])
                ins.then_inc(t_free, 1)

            def head_state(hd, m):
                for d in range(2):
                    bank = o_whole()
                    dve.wait_ge(o_free, O_.at(-2) if m > 0 else O_.at(-1))
                    ch = 3 - m if d else m
                    old = ctx_state[:, hd, d, :] if m == 0 else states[:, d, m - 1, :]
                    ins = nc.vector.scalar_tensor_tensor(out=states[:, d, m, :], in0=old, scalar=dec[:, d, ch:ch + 1],
                                                         in1=bank[:, 0:DV], op0=ALU.mult, op1=ALU.add)
                    ins.then_inc(o_free, 1)

            def head_gate(hd):
                dve.wait_ge(a_full, F.at(1))
                F.n += 1
                dve.wait_ge(osq_ready, TT * (hd + 1))
                inverse_rms(4, TT, DV)
                bank = freed()
                for t in range(TT):
                    ins = nc.vector.scalar_tensor_tensor(out=o_tmp[:, t, :], in0=bank[:, t * DV:(t + 1) * DV],
                                                         scalar=rstd[:, 4 + t:5 + t], in1=gla_g[:, :], op0=ALU.mult, op1=ALU.mult)
                ins.then_inc(a_free, 1)
                dve.wait_ge(a_free, FREE.at())
                for t in range(TT):
                    dst = r_tok[:, t, hd * DV:(hd + 1) * DV]
                    nc.vector.tensor_tensor(dst, dst, o_tmp[:, t, :], ALU.mult).then_inc(gated, 1)

            ad.slabs = 4 * START_UNITS
            for n, (what, n0, shared) in enumerate(MIX):
                for q in range(KC // KS):
                    split()
                    if ad.turned():
                        ada_add()
                    if n == 0:
                        log_gate(2 * q)
                        log_gate(2 * q + 1)
                    if q == 3:
                        tiles = 2 * TT if shared else TT
                        assert FREE.n == A_MIX[n]
                        for t in range(tiles):
                            tile_ends(t == tiles - 1)
                            bank = freed()
                            if what == "k":
                                ins = nc.vector.tensor_copy((k_tok if t < TT else kc_tok)[:, t % TT, :], bank[:, :])
                            elif what == "v":
                                ins = nc.vector.tensor_copy((v_tok if t < TT else vc_tok)[:, t % TT, n0 - V_OFF:n0 - V_OFF + NW], bank[:, :])
                            elif what == "q":
                                ins = nc.vector.tensor_scalar(q_tok[:, t, :], bank[:, :], DK ** -0.5, None, ALU.mult)
                            elif what == "r":
                                SIG.n += 1
                                dve.wait_ge(sig_ready, SIG.n)
                                dst = r_tok[:, t, n0 - R_OFF:n0 - R_OFF + NW]
                                ins = nc.vector.tensor_tensor(dst, dst, bank[:, :], ALU.mult)
                            else:
                                ins = nc.vector.tensor_copy(f_tok[:, t, n0 - F_OFF:n0 - F_OFF + NW], bank[:, :])
                            ins.then_inc(a_free, 1)
                    if n == 0 and q == 3:
                        nc.vector.memset(att, 0.0)
                    if n == 1 and q == 2:
                        finish_log_gates()
                    if n == 3 and q == 0:
                        tails(kc_tail, kc_tok)
                    if n == 3 and q == 1:
                        for hd in range(HEADS):
                            nc.vector.tensor_copy(ctx_state[:, hd, :, :].rearrange("p d v -> p (d v)"),
                                                  o_whole()[:, :]).then_inc(o_free, 1)
                    if n == 3 and q == 2:
                        tails(k_tail, k_tok)
                    if n == 4 and q == 0:
                        for dst in (qT, kT):
                            for t in range(TT):
                                t_whole()
                                nc.vector.tensor_copy(dst[:, :, t * P:(t + 1) * P],
                                                      T[:, :].rearrange("p (k s) -> p k s", k=HEADS)).then_inc(t_free, 1)
                    if n >= 4:
                        hd = n - 4
                        if q == 0:
                            head_decays(hd)
                        if q == 1:
                            head_mask(hd)
                            head_state(hd, 0)
                        if q == 2:
                            head_state(hd, 1)
                            head_state(hd, 2)
                        if q == 3:
                            head_gate(hd)
                    if shared:
                        ada_sum(ADA_MIX[4 * n + q])
                        ad.work(ADA_MIX[4 * n + q])
                    elif ad.work(ADA_MIX[4 * n + q]):
                        ada_copy()

            Y = Tally()

            def y_lo(k0):
                t_whole()
                Y.n += 1
                dve.wait_ge(y_hi, Y.n)
                nc.vector.tensor_tensor(a_lo[:, k0:k0 + 2, :], T[:, :].rearrange("p (k s) -> p k s", k=2),
                                        a_hi[:, k0:k0 + 2, :].bitcast(F32), ALU.subtract).then_inc(t_free, 1)

            def fnet(g):
                for dc in range(2):
                    bank = o_whole()
                    nc.vector.tensor_copy(fn_cs[:, g % 2, dc, 0:SEQ], bank[:, 0:SEQ])
                    nc.vector.tensor_scalar(fn_cs[:, g % 2, dc, SEQ:2 * SEQ], bank[:, SEQ:2 * SEQ], -1.0, None,
                                            ALU.mult).then_inc(o_free, 1)
                y_lo(8 + 2 * g)

            fnet(0)
            fnet(1)
            for j in range(4):
                y_lo(2 * j)
            diagonal(0, GATE_MIX, 0)
            for m in range(4):
                for q in range(KC // KS):
                    split()
                    if ad.turned():
                        ada_add()
                    if q == 0:
                        gate_quarter(0, GATE_MIX, m)
                    if m == 0 and q == 3:
                        dve.wait_ge(h_landed, 32)
                        for t in range(TT):
                            ins = nc.vector.tensor_tensor(h[:, t, :], h[:, t, :], pe_out[:, t, :], ALU.add)
                        chained(ins)
                        dve.wait_ge(t_free, T_.at())
                    if q == 3:
                        for t in range(TT):
                            residual(t, m)
                    if ad.work(ADA_OUT[4 * m + q]):
                        ada_copy()
                    if m == 0 and q < 2:
                        fnet(2 + q)
                        if ad.work(FNET_ADA):
                            ada_copy()
            if ad.turned():
                ada_add()

            def ffn(layer):
                dve.wait_ge(h_ready, 4 * TT * (2 * layer + 1))
                dve.wait_ge(t_free, T_.at())
                normed(acc, h, 0)
                set_gain(layer, SCALE_FFN, V_FFNG + layer * KC)
                norm_out(a_hi, a_lo, modc(layer, SHIFT_FFN), a32_ffn)

                def block_in(offset, head=False):
                    for n in range(8):
                        split()
                        if head and n == 1:
                            nc.vector.memset(acc, 0.0)
                        if layer == 0 and ad.turned():
                            ada_add(offset)
                        if n == 3:
                            D_.n += 1
                        if n == 7:
                            for t in range(TT):
                                dve.wait_ge(sg_ready, SG.at(1))
                                SG.n += 1
                                tile_ends(t == TT - 1)
                                ins = nc.vector.tensor_tensor(hid_tok[:, t, :], A[2 + t][:, :], sg[:, t, :], ALU.mult)
                            ins.then_inc(a_free, 4)
                            FREE.n += 4
                        if layer == 0:
                            ada_sum(ADA_FFN[n])
                            ad.work(ADA_FFN[n])

                def hidden_lo():
                    for t, bank in enumerate((T, AD)):
                        t_whole()
                        dve.wait_ge(hid_hi_ready, H.at(1))
                        H.n += 1
                        nc.vector.tensor_tensor(hid_lo[:, :, t * P:(t + 1) * P], bank[:, :].rearrange("p (k s) -> p k s", k=KS),
                                                hid_hi[:, :, t * P:(t + 1) * P].bitcast(F32), ALU.subtract).then_inc(t_free, 1)

                def o_ends(t):
                    tile_ends(t == TT - 1)
                    O_.n += 1
                    return O[t]

                block_in(None, head=True)
                hidden_lo()
                steps = [(S, 12), (W, 12), (D_, 6), (SG, 2), (FREE, 4), (H, 2), (O_, 8)]
                steps += [(T_, 3), (U, 4), (V, 16), (G, 1)] if layer == 0 else [(T_, 2)]
                for i in loop(dve, FB - 1, *steps):
                    block_in(i * 4 + 24 * 4)
                    for m in range(4):
                        split()
                        for t in range(TT):
                            cols = slice(m * NW, (m + 1) * NW)
                            bank = o_ends(t)
                            nc.vector.tensor_tensor(acc[:, t, cols], acc[:, t, cols], bank[:, :], ALU.add).then_inc(o_free, 1)
                    hidden_lo()
                diagonal(layer, GATE_FFN, 0)
                for m in range(4):
                    split()
                    for t in range(TT):
                        cols = slice(m * NW, (m + 1) * NW)
                        bank = o_ends(t)
                        nc.vector.tensor_tensor(acc[:, t, cols], acc[:, t, cols], bank[:, :], ALU.add).then_inc(o_free, 1)
                        dve.wait_ge(o_free, O_.at())
                        if t == 0:
                            gate_quarter(layer, GATE_FFN, m)
                            dve.wait_ge(t_free, T_.at())
                        chained(nc.vector.tensor_tensor(acc[:, t, cols], acc[:, t, cols], gate_bc[:, cols], ALU.mult))
                        nc.vector.tensor_tensor(h[:, t, cols], h[:, t, cols], acc[:, t, cols], ALU.add).then_inc(h_ready, 1)

            ffn(0)

            dve.wait_ge(t_free, T_.at())
            normed(acc, h, 0)
            set_gain(1, SCALE_MIX, V_MIXG + KC)
            nc.vector.memset(uT[:, :, 0:HALO], 0.0)
            nc.vector.memset(uT[:, :, HALO + SEQ:], 0.0)
            norm_out(a_hi, a_lo, modc(1, SHIFT_MIX), a32_ffn)
            C, PR = Tally(), Tally()

            def taps(piece, b_col, first, last, order=CONV_LIST):
                for n in range(first, last):
                    m, tap = order[n]
                    p = piece(m)
                    w = w_dw[:, p, tap:tap + 1].rearrange("p a b -> p (a b)")
                    dst, src = conv_v[:, p, :], uT[:, p, tap:tap + SEQ]
                    if n == 0:
                        dve.wait_ge(t_free, T_.at())
                    if tap == 0:
                        nc.vector.tensor_scalar(dst, src, w, b_col(m), ALU.mult, ALU.add).then_inc(conv_dve, 1)
                    else:
                        before = n - order.index((m, tap - 1))
                        dve.wait_ge(conv_dve, C.at(1 - before))
                        nc.vector.scalar_tensor_tensor(out=dst, in0=src, scalar=w, in1=dst, op0=ALU.mult,
                                                       op1=ALU.add).then_inc(conv_dve, 1)
                    C.n += 1

            def u_tile(dst_pieces, t):
                t_whole()
                nc.vector.tensor_copy(uT[:, dst_pieces, HALO + t * P:HALO + (t + 1) * P],
                                      (T, AD)[t][:, :].rearrange("p (k s) -> p k s", k=KS)).then_inc(t_free, 1)

            def pw1_block(offsets, before, piece, b_col):
                for n in range(8):
                    split()
                    if ad.turned():
                        ada_add(offsets[0 if n == 0 else 1])
                    if before is not None:
                        if n == 0:
                            u_tile(before, 0)
                            u_tile(before, 1)
                        taps(piece, b_col, *share(len(CONV_LIST), n))
                    if n == 7:
                        for t in range(TT):
                            dve.wait_ge(sg_ready, SG.at(1))
                            SG.n += 1
                            tile_ends(t == TT - 1)
                            ins = nc.vector.tensor_tensor(hid_tok[:, t, :], A[t][:, :], sg[:, t, :], ALU.mult)
                        ins.then_inc(a_free, 4)
                        FREE.n += 4
                    if before is not None and n == 7:
                        dve.wait_ge(prod_added, PR.at(PRODS))
                        dve.wait_ge(conv_dve, C.at())
                        v = conv_v[:, piece(2), :]
                        nc.vector.tensor_tensor(v, v, pool_acc2[:, None, :], ALU.add).then_inc(conv_dve, 1)
                        C.n += 1
                        PR.n += PRODS
                    if n == 3:
                        D_.n += 1
                    if ad.work(ADA_PW1[n]):
                        ada_copy()

            assert ad.slabs % 4 == 0
            pw1_block((None, None), None, None, None)
            for i in loop(dve, 3, (S, 8), (W, 8), (D_, 2), (T_, 4), (SG, 2), (FREE, 4), (USED, 8), (U, 8), (G, 2),
                          (C, len(CONV_LIST) + 1), (PR, PRODS)):
                pw1_block((i * 8 + 35 * 4, i * 8 + 36 * 4), bass.ds(i * KS, KS),
                          lambda m: bass.ds(i * KS + m, 1), lambda m: vecs[:, bass.ds(i * KS + (V_BDW + m), 1)])
            if ad.turned():
                ada_add()
            for t in range(TT):
                u_tile(slice(KC - KS, KC), t)
            order = [(m, tap) for tap in range(CONV_W) for m in range(KS - 1)]
            done = 0
            for last, ada_step in ((33, ada_copy), (38, ada_add), (66, ada_copy), (71, ada_add), (len(order), None)):
                taps(lambda m: slice(KC - KS + m, KC - KS + m + 1),
                     lambda m: vecs[:, V_BDW + KC - KS + m:V_BDW + KC - KS + m + 1], done, last, order)
                done = last
                if ada_step:
                    ada_step()
            ad.work(4 * (TAIL_UNITS - 1))
            ad.turned()

            def over_channels(v):
                return v[:, None, :].to_broadcast([P, KS, SEQ])

            bank = o_whole()
            nc.vector.tensor_scalar(mean_bc, bank[:, 0:SEQ], 1.0 / D, None, ALU.mult).then_inc(o_free, 1)
            dve.wait_ge(o_free, O_.at())
            for g in range(4):
                v = conv_v[:, KS * g:KS * (g + 1), :]
                nc.vector.tensor_tensor(v, v, over_channels(mean_bc), ALU.subtract).then_inc(xc_ready, 1)
            bank = o_whole()
            nc.vector.tensor_scalar(rstd_bc, bank[:, 0:SEQ], 1.0 / D, EPS, ALU.mult, ALU.add).then_inc(o_free, 1)
            dve.wait_ge(o_free, O_.at())
            inverse_root(rstd_bc)
            for g in range(4):
                v = conv_v[:, KS * g:KS * (g + 1), :]
                nc.vector.tensor_tensor(v, v, over_channels(rstd_bc), ALU.mult).then_inc(yn_ready, 1)
            ada_copy()
            ad.work(4)
            for j in range(KC // 2):
                dve.wait_ge(ln_hi, j + 1)
                nc.vector.tensor_tensor(a_lo[:, 2 * j:2 * j + 2, :], a32_ffn[:, j % 2, :, :],
                                        a_hi[:, 2 * j:2 * j + 2, :].bitcast(F32), ALU.subtract).then_inc(ln_lo, 1)
            diagonal(1, GATE_MIX, 0)
            for m in range(4):
                for q in range(KC // KS):
                    split()
                    if ad.turned():
                        ada_add()
                    if q == 0:
                        gate_quarter(1, GATE_MIX, m)
                        dve.wait_ge(t_free, T_.at())
                    if q == 3:
                        for t in range(TT):
                            residual(t, m)
                    if ad.work(ADA_PW2[q]):
                        ada_copy()
            if ad.turned():
                ada_add()
            ffn(1)

            h_squares()
            inverse_rms(0, TT, D)
            dve.wait_ge(fin_landed, 16)
            for t in range(TT):
                chained(nc.vector.tensor_scalar(h[:, t, :], h[:, t, :], rstd[:, t:t + 1], None, ALU.mult))
                nc.vector.tensor_tensor(h[:, t, :], h[:, t, :], fin_g, ALU.mult).then_inc(result_ready, 1)


_INS = ['x', 'c', 'ctx', 'c_ctx', 'ada_w', 'ada_b', 'norm_mix_g', 'norm_ffn_g', 'ffn_w_in', 'ffn_w_out', 'gm_w_in',
        'gla_gate_w_fwd', 'gla_gate_b_fwd', 'gla_gate_w_bwd', 'gla_gate_b_bwd', 'gla_norm_g', 'gm_w_out', 'cv_w_pw1',
        'cv_b_pw1', 'cv_w_dw', 'cv_b_dw', 'cv_ln_g', 'cv_ln_b', 'cv_w_pw2', 'cv_b_pw2', 'final_norm_g']
_OUTS = [((1, SEQ, D), 'float32')]


def _constants():
    import numpy as np
    grid_w = 64
    r = np.repeat(np.arange(SEQ // grid_w, dtype=np.float32), grid_w)
    col = np.tile(np.arange(grid_w, dtype=np.float32), SEQ // grid_w)
    nq = D // 4
    omega = (1.0 / (np.float32(10000.0) ** (np.arange(nq, dtype=np.float32) / np.float32(nq)))).astype(np.float32)
    ar, ac = r[:, None] * omega[None, :], col[:, None] * omega[None, :]
    pos = np.concatenate([np.sin(ar), np.cos(ar), np.sin(ac), np.cos(ac)], axis=-1).astype(np.float32)

    j, t = np.arange(P)[:, None], np.arange(P)[None, :]
    near = j // CHUNK == t // CHUNK
    norm = 1.0 / 16.0
    mats = [j == t, norm * (near & (j <= t)), norm * (near & (j >= t)), norm * (near & (j > t)),
            norm * (near & (j < t)), norm * (j > t), norm * (j < t), norm * np.ones((P, P))]
    pick = np.stack([np.arange(P) % 32 == 0, np.arange(P) % 32 == 1], axis=1)
    matrices = np.concatenate([np.asarray(m, np.float32) for m in mats + [pick]], axis=1)

    n = np.arange(SEQ)
    angle = 2 * np.pi * (np.outer(n, n) % SEQ) / SEQ
    cos, sin = np.cos(angle) / 16.0, np.sin(angle) / 16.0
    dft = np.concatenate([cos, sin], axis=1).astype(np.float32)
    return {'pos_embed': pos, 'matrices': np.ascontiguousarray(matrices), 'dft': dft}


def kernel(**inputs):
    import numpy as _np
    import concourse.bacc as _bacc
    from concourse import mybir as _mybir
    from concourse.bass_utils import run_bass_kernel_spmd as _run

    nc = _bacc.Bacc("TRN2", target_bir_lowering=False, num_devices=1)
    arrays, args = {}, []
    given = {name: _np.ascontiguousarray(inputs[name]) for name in _INS}
    for name, a in list(given.items()) + list(_constants().items()):
        arrays[f"in_{name}_dram"] = a
        args.append(nc.dram_tensor(f"in_{name}_dram", a.shape, _mybir.dt.from_np(a.dtype), kind="ExternalInput").ap())
    for i, (shape, dtype) in enumerate(_OUTS):
        dt = _mybir.dt.from_np(_np.dtype(dtype))
        args.append(nc.dram_tensor(f"out_{i}_dram", shape, dt, kind="ExternalOutput").ap())
    program(nc, *args)
    r = _run(nc, [arrays], core_ids=[0])
    return r.results[0]["out_0_dram"]
```
